# Optimizing a Trainium2 kernel written in Bass

```python
import jax, jax.numpy as jnp
from jax import lax
import numpy as np

D_MODEL = 1024
BATCH = 1
SEQ = 512
DEPTH = 1

SSM_HEADS = 16
SSM_HEAD_DIM = 64
SSM_WIDTH = SSM_HEADS * SSM_HEAD_DIM
SSM_GROUPS = 2
SSM_STATE = 128
CONV_WIDTH = 4
CHUNK = 128
CONV_DIM = SSM_WIDTH + 2 * SSM_GROUPS * SSM_STATE
ATT_HEADS = 16
ATT_HEAD_DIM = 64
ATT_WIDTH = ATT_HEADS * ATT_HEAD_DIM
Q_BLOCK = 128
MIX_WIDTH = SSM_WIDTH + ATT_WIDTH
D_FF = 4 * D_MODEL
SPLITS = [SSM_WIDTH,
          SSM_WIDTH + CONV_DIM,
          SSM_WIDTH + CONV_DIM + SSM_HEADS,
          SSM_WIDTH + CONV_DIM + SSM_HEADS + ATT_WIDTH,
          SSM_WIDTH + CONV_DIM + SSM_HEADS + 2 * ATT_WIDTH,
          SSM_WIDTH + CONV_DIM + SSM_HEADS + 3 * ATT_WIDTH]
IN_COLS = SPLITS[-1] + ATT_HEADS
DEEPNORM_ALPHA = (2.0 * DEPTH) ** 0.25
DEEPNORM_BETA = (8.0 * DEPTH) ** -0.25
LN_EPS = 1e-5
RMS_EPS = 1e-5


def layer_norm(x, g, b):
    xf = x.astype(jnp.float32)
    mu = jnp.mean(xf, axis=-1, keepdims=True)
    var = jnp.mean(jnp.square(xf - mu), axis=-1, keepdims=True)
    return ((xf - mu) * lax.rsqrt(var + LN_EPS) * g + b).astype(x.dtype)

def rms_norm(x, w):
    xf = x.astype(jnp.float32)
    return xf * lax.rsqrt(jnp.mean(xf * xf, axis=-1, keepdims=True) + RMS_EPS) * w

def causal_depthwise_conv(u, w, b):
    out = lax.conv_general_dilated(
        u, w[:, None, :].astype(u.dtype), window_strides=(1,),
        padding=[(CONV_WIDTH - 1, 0)], dimension_numbers=('NWC', 'WIO', 'NWC'),
        feature_group_count=u.shape[-1])
    return out + b

def segsum(a):
    cs = jnp.cumsum(a, axis=-1)
    diff = cs[..., :, None] - cs[..., None, :]
    t = a.shape[-1]
    mask = jnp.tril(jnp.ones((t, t), dtype=bool))
    return jnp.where(mask, diff, -jnp.inf)

def ssd_chunked(xh, dt, A, Bm, Cm):
    b, s, h, p = xh.shape
    g, n = Bm.shape[-2], Bm.shape[-1]
    e = h // g
    nc = s // CHUNK
    xc = (xh.astype(jnp.float32) * dt[..., None]).reshape(b, nc, CHUNK, g, e, p)
    Bc = Bm.astype(jnp.float32).reshape(b, nc, CHUNK, g, n)
    Cc = Cm.astype(jnp.float32).reshape(b, nc, CHUNK, g, n)
    a = (dt * A).reshape(b, nc, CHUNK, g, e).transpose(0, 3, 4, 1, 2)
    a_cs = jnp.cumsum(a, axis=-1)
    decay_in = jnp.exp(segsum(a))
    cb = jnp.einsum('bclgn,bcsgn->bgcls', Cc, Bc)
    scores = cb[:, :, None] * decay_in
    y_diag = jnp.einsum('bgecls,bcsgep->bclgep', scores, xc)
    decay_to_end = jnp.exp(a_cs[..., -1:] - a_cs).transpose(0, 3, 4, 1, 2)
    states = jnp.einsum('bclgn,bclgep->bcgepn', Bc, xc * decay_to_end[..., None])
    chunk_tot = jnp.pad(a_cs[..., -1], [(0, 0), (0, 0), (0, 0), (1, 0)])
    decay_chunk = jnp.exp(segsum(chunk_tot))
    states = jnp.concatenate([jnp.zeros_like(states[:, :1]), states], axis=1)
    new_states = jnp.einsum('bgezc,bcgepn->bzgepn', decay_chunk, states)
    prev_states = new_states[:, :-1]
    decay_out = jnp.exp(a_cs).transpose(0, 3, 4, 1, 2)
    y_off = jnp.einsum('bclgn,bcgepn->bclgep', Cc, prev_states) * decay_out[..., None]
    return (y_diag + y_off).reshape(b, s, h, p)

def forgetting_attention(q, k, v, log_f):
    s, d = q.shape[1], q.shape[-1]
    scale = d ** -0.5
    cum = jnp.cumsum(log_f, axis=1).transpose(0, 2, 1)
    outs = []
    for i in range(s // Q_BLOCK):
        q0, q1 = i * Q_BLOCK, (i + 1) * Q_BLOCK
        logits = jnp.einsum('bqhd,bkhd->bhqk', q[:, q0:q1], k[:, :q1],
                            preferred_element_type=jnp.float32) * scale
        logits = logits + (cum[:, :, q0:q1, None] - cum[:, :, None, :q1])
        mask = jnp.arange(q0, q1)[:, None] >= jnp.arange(q1)[None, :]
        logits = jnp.where(mask, logits, -jnp.inf)
        probs = jax.nn.softmax(logits, axis=-1)
        outs.append(jnp.einsum('bhqk,bkhd->bqhd', probs.astype(v.dtype), v[:, :q1]))
    return jnp.concatenate(outs, axis=1)

def hybrid_mixer(h, w_in, conv_w, conv_b, dt_bias, a_log, d_skip, ssm_norm_w, f_bias,
                 attn_norm_w, w_out):
    b, s, _ = h.shape
    proj = jnp.einsum('bsd,dk->bsk', h, w_in)
    z, xbc, dt_raw, q, k, v, f_raw = jnp.split(proj, SPLITS, axis=-1)
    xbc = jax.nn.silu(causal_depthwise_conv(xbc, conv_w, conv_b))
    xs, Bm, Cm = jnp.split(xbc, [SSM_WIDTH, SSM_WIDTH + SSM_GROUPS * SSM_STATE], axis=-1)
    xs = xs.reshape(b, s, SSM_HEADS, SSM_HEAD_DIM)
    Bm = Bm.reshape(b, s, SSM_GROUPS, SSM_STATE)
    Cm = Cm.reshape(b, s, SSM_GROUPS, SSM_STATE)
    dt = jax.nn.softplus(dt_raw.astype(jnp.float32) + dt_bias)
    A = -jnp.exp(a_log.astype(jnp.float32))
    y = ssd_chunked(xs, dt, A, Bm, Cm) + d_skip[:, None] * xs
    y_ssm = rms_norm(y.reshape(b, s, SSM_WIDTH) * jax.nn.silu(z), ssm_norm_w)
    q = q.reshape(b, s, ATT_HEADS, ATT_HEAD_DIM)
    k = k.reshape(b, s, ATT_HEADS, ATT_HEAD_DIM)
    v = v.reshape(b, s, ATT_HEADS, ATT_HEAD_DIM)
    log_f = jax.nn.log_sigmoid(f_raw.astype(jnp.float32) + f_bias)
    y_att = forgetting_attention(q, k, v, log_f).reshape(b, s, ATT_WIDTH)
    y_att = rms_norm(y_att, attn_norm_w)
    y_mix = jnp.concatenate([y_ssm, y_att.astype(y_ssm.dtype)], axis=-1)
    return jnp.einsum('bsk,kd->bsd', y_mix.astype(h.dtype), w_out)

def first_inputs(seed: int = 0) -> dict:
    key = jax.random.key(seed)
    ks = jax.random.split(key, 24)
    f32 = jnp.float32
    nrm = lambda k, shape, s: jax.random.normal(k, shape, f32) * s
    dt0 = jnp.exp(jax.random.uniform(ks[6], (DEPTH, SSM_HEADS), f32,
                                     np.log(1e-3).astype(np.float32), np.log(1e-1).astype(np.float32)))
    return {
        "x": nrm(ks[0], (BATCH, SEQ, D_MODEL), 1.0),
        "c": nrm(ks[1], (BATCH, D_MODEL), 1.0),
        "w_ada": nrm(ks[2], (DEPTH, D_MODEL, 6 * D_MODEL), 0.5 * D_MODEL ** -0.5),
        "b_ada": nrm(ks[3], (DEPTH, 6 * D_MODEL), 0.01),
        "w_in": nrm(ks[4], (DEPTH, D_MODEL, IN_COLS), D_MODEL ** -0.5),
        "conv_w": nrm(ks[5], (DEPTH, CONV_WIDTH, CONV_DIM), CONV_WIDTH ** -0.5),
        "conv_b": nrm(ks[7], (DEPTH, CONV_DIM), 0.01),
        "dt_bias": dt0 + jnp.log(-jnp.expm1(-dt0)),
        "a_log": jnp.log(jax.random.uniform(ks[8], (DEPTH, SSM_HEADS), f32, 1.0, 16.0)),
        "d_skip": 1.0 + nrm(ks[9], (DEPTH, SSM_HEADS), 0.1),
        "ssm_norm_w": 1.0 + nrm(ks[10], (DEPTH, SSM_WIDTH), 0.05),
        "f_bias": jax.random.uniform(ks[11], (DEPTH, ATT_HEADS), f32, 1.0, 4.0),
        "attn_norm_w": 1.0 + nrm(ks[12], (DEPTH, ATT_WIDTH), 0.05),
        "w_out": nrm(ks[13], (DEPTH, MIX_WIDTH, D_MODEL), DEEPNORM_BETA * MIX_WIDTH ** -0.5),
        "ln1_g": 1.0 + nrm(ks[14], (DEPTH, D_MODEL), 0.05),
        "ln1_b": nrm(ks[15], (DEPTH, D_MODEL), 0.01),
        "w_ff_in": nrm(ks[16], (DEPTH, D_MODEL, D_FF), D_MODEL ** -0.5),
        "w_ff_out": nrm(ks[17], (DEPTH, D_FF, D_MODEL), DEEPNORM_BETA * D_FF ** -0.5),
        "ln2_g": 1.0 + nrm(ks[18], (DEPTH, D_MODEL), 0.05),
        "ln2_b": nrm(ks[19], (DEPTH, D_MODEL), 0.01),
    }

def first_block(x, c, w_ada, b_ada, w_in, conv_w, conv_b, dt_bias, a_log, d_skip, ssm_norm_w,
              f_bias, attn_norm_w, w_out, ln1_g, ln1_b, w_ff_in, w_ff_out, ln2_g, ln2_b):
    c_act = jax.nn.silu(c)
    for l in range(DEPTH):
        mod = jnp.einsum('bd,de->be', c_act, w_ada[l]) + b_ada[l]
        sh1, sc1, g1, sh2, sc2, g2 = [m[:, None, :] for m in jnp.split(mod, 6, axis=-1)]
        h = x * (1.0 + sc1) + sh1
        y = hybrid_mixer(h, w_in[l], conv_w[l], conv_b[l], dt_bias[l], a_log[l], d_skip[l],
                         ssm_norm_w[l], f_bias[l], attn_norm_w[l], w_out[l])
        x = layer_norm(DEEPNORM_ALPHA * x + (1.0 + g1) * y, ln1_g[l], ln1_b[l])
        h = x * (1.0 + sc2) + sh2
        ff = jnp.einsum('bsf,fd->bsd',
                        jnp.square(jax.nn.relu(jnp.einsum('bsd,df->bsf', h, w_ff_in[l]))),
                        w_ff_out[l])
        x = layer_norm(DEEPNORM_ALPHA * x + (1.0 + g2) * ff, ln2_g[l], ln2_b[l])
    return x


HEAD_DIM = 64
N_Q_HEADS = 8
N_KV_HEADS = 2
Q_REP = N_Q_HEADS // N_KV_HEADS
ATTN_WIDTH = N_Q_HEADS * HEAD_DIM
KV_WIDTH = N_KV_HEADS * HEAD_DIM
WINDOW = 128
ATTN_BLOCK = 128
N_GMLP_GROUPS = 8
GMLP_WIDTH = D_MODEL - ATTN_WIDTH
GMLP_GROUP_DIM = GMLP_WIDTH // N_GMLP_GROUPS
MIX_WIDTH_2 = ATTN_WIDTH + GMLP_WIDTH
IN_WIDTH = ATTN_WIDTH + 2 * KV_WIDTH + 2 * GMLP_WIDTH
N_EXPERTS = 32
TOP_K = 4
D_FF_2 = D_MODEL
SWIGLU_LIMIT = 7.0
SWIGLU_ALPHA = 1.702
MOE_BLOCK = 128
DEEPNORM_ALPHA_2 = (2.0 * DEPTH) ** 0.25
DEEPNORM_BETA_2 = (8.0 * DEPTH) ** -0.25
NEG_INF = -1e30


def layer_norm_2(x, g, b):
    xf = x.astype(jnp.float32)
    mu = jnp.mean(xf, axis=-1, keepdims=True)
    xc = xf - mu
    var = jnp.mean(xc * xc, axis=-1, keepdims=True)
    return (xc * lax.rsqrt(var + LN_EPS)).astype(x.dtype) * g + b

def sliding_window_attention(q, k, v, sinks):
    B, S = q.shape[:2]
    nb = S // ATTN_BLOCK
    q = q.reshape(B, nb, ATTN_BLOCK, N_KV_HEADS, Q_REP, HEAD_DIM)
    k = k.reshape(B, nb, ATTN_BLOCK, N_KV_HEADS, HEAD_DIM)
    v = v.reshape(B, nb, ATTN_BLOCK, N_KV_HEADS, HEAD_DIM)

    def band(t):
        prev = jnp.pad(t[:, :-1], ((0, 0), (1, 0), (0, 0), (0, 0), (0, 0)))
        return jnp.concatenate([prev, t], axis=2)

    kb, vb = band(k), band(v)
    scores = jnp.einsum('bnqgrd,bnkgd->bngrqk', q, kb).astype(jnp.float32) * (HEAD_DIM ** -0.5)
    t_idx = jnp.arange(ATTN_BLOCK)[:, None]
    s_idx = jnp.arange(2 * ATTN_BLOCK)[None, :]
    diff = t_idx + ATTN_BLOCK - s_idx
    in_band = (diff >= 0) & (diff < WINDOW)
    blk = jnp.arange(nb)[:, None, None]
    valid = in_band[None] & ((blk * ATTN_BLOCK - ATTN_BLOCK + s_idx[None]) >= 0)
    scores = jnp.where(valid[None, :, None, None], scores, NEG_INF)
    sink = sinks.astype(jnp.float32).reshape(N_KV_HEADS, Q_REP)[None, None, :, :, None, None]
    sink = jnp.broadcast_to(sink, scores.shape[:-1] + (1,))
    probs = jax.nn.softmax(jnp.concatenate([scores, sink], axis=-1), axis=-1)[..., :-1]
    out = jnp.einsum('bngrqk,bnkgd->bnqgrd', probs.astype(v.dtype), vb)
    return out.reshape(B, S, ATTN_WIDTH)

def chunked_spatial_gating(u, g, ln_g, ln_b, w_s, b_s):
    B, S = u.shape[:2]
    nc = S // CHUNK
    u = jax.nn.gelu(u)
    g = jax.nn.gelu(g).reshape(B, S, N_GMLP_GROUPS, GMLP_GROUP_DIM)
    g = layer_norm_2(g, ln_g.reshape(N_GMLP_GROUPS, GMLP_GROUP_DIM), ln_b.reshape(N_GMLP_GROUPS, GMLP_GROUP_DIM))
    g = g.reshape(B, nc, CHUNK, N_GMLP_GROUPS, GMLP_GROUP_DIM)
    causal = jnp.tril(jnp.ones((CHUNK, CHUNK), dtype=bool))
    w = jnp.where(causal[None], w_s, jnp.zeros_like(w_s))
    mixed = jnp.einsum('gts,bcsgd->bctgd', w, g) + b_s.T[None, None, :, :, None]
    return u * mixed.reshape(B, S, GMLP_WIDTH)

def token_mixer(x, w_in, b_in, sinks, ln_v_g, ln_v_b, w_spatial, b_spatial, w_out, b_out):
    proj = x @ w_in + b_in
    o1 = ATTN_WIDTH
    o2 = o1 + KV_WIDTH
    o3 = o2 + KV_WIDTH
    o4 = o3 + GMLP_WIDTH
    q, k, v = proj[..., :o1], proj[..., o1:o2], proj[..., o2:o3]
    u, g = proj[..., o3:o4], proj[..., o4:]
    attn = sliding_window_attention(q, k, v, sinks)
    sgu = chunked_spatial_gating(u, g, ln_v_g, ln_v_b, w_spatial, b_spatial)
    return jnp.concatenate([attn, sgu], axis=-1) @ w_out + b_out

def routed_experts(x, w_router, b_router, w_gate, b_gate, w_up, b_up, w_down, b_down):
    B, S, D = x.shape
    T = B * S
    TK = T * TOP_K
    xt = x.reshape(T, D)
    logits = (xt @ w_router + b_router).astype(jnp.float32)
    top_vals, top_idx = lax.top_k(logits, TOP_K)
    gates = jax.nn.softmax(top_vals, axis=-1).astype(x.dtype)
    flat_e = top_idx.reshape(-1)
    flat_tok = jnp.arange(TK, dtype=jnp.int32) // TOP_K
    order = jnp.argsort(flat_e)
    sorted_e = flat_e[order]
    counts = jnp.bincount(flat_e, length=N_EXPERTS)
    start = jnp.cumsum(counts) - counts
    padded = (counts + MOE_BLOCK - 1) // MOE_BLOCK * MOE_BLOCK
    padded_end = jnp.cumsum(padded)
    padded_start = padded_end - padded
    dest = padded_start[sorted_e] + jnp.arange(TK, dtype=jnp.int32) - start[sorted_e]
    n_blocks = TK // MOE_BLOCK + N_EXPERTS
    n_rows = n_blocks * MOE_BLOCK
    row_tok = jnp.full((n_rows,), T, dtype=jnp.int32).at[dest].set(flat_tok[order])
    row_gate = jnp.zeros((n_rows,), x.dtype).at[dest].set(gates.reshape(-1)[order])
    block_e = jnp.minimum(
        jnp.searchsorted(padded_end, jnp.arange(n_blocks, dtype=padded_end.dtype) * MOE_BLOCK, side='right'),
        N_EXPERTS - 1)
    x_rows = jnp.concatenate([xt, jnp.zeros((1, D), xt.dtype)], axis=0)[row_tok]
    x_rows = x_rows.reshape(n_blocks, MOE_BLOCK, D)

    def expert_block(args):
        xb, e = args
        gt = jnp.minimum(xb @ w_gate[e] + b_gate[e], SWIGLU_LIMIT)
        up = jnp.clip(xb @ w_up[e] + b_up[e], -SWIGLU_LIMIT, SWIGLU_LIMIT)
        hid = gt * jax.nn.sigmoid(SWIGLU_ALPHA * gt) * (up + 1.0)
        return hid @ w_down[e] + b_down[e]

    y_rows = lax.map(expert_block, (x_rows, block_e)).reshape(n_rows, D)
    out = jnp.zeros((T + 1, D), x.dtype).at[row_tok].add(y_rows * row_gate[:, None])[:T]
    return out.reshape(B, S, D)

def second_inputs(seed: int = 0) -> dict:
    key = jax.random.key(seed)
    ks = jax.random.split(key, 24)
    f32 = jnp.float32

    def nrm(k, shape, scale):
        return jax.random.normal(k, (DEPTH,) + shape, f32) * scale

    x = jax.random.normal(ks[0], (BATCH, SEQ, D_MODEL), f32)
    col_scale = jnp.concatenate([
        jnp.ones((ATTN_WIDTH + KV_WIDTH,), f32),
        jnp.full((KV_WIDTH,), DEEPNORM_BETA_2, f32),
        jnp.full((GMLP_WIDTH,), DEEPNORM_BETA_2, f32),
        jnp.ones((GMLP_WIDTH,), f32)])
    w_in = nrm(ks[1], (D_MODEL, IN_WIDTH), D_MODEL ** -0.5) * col_scale
    b_in = nrm(ks[2], (IN_WIDTH,), 0.02)
    sinks = nrm(ks[3], (N_Q_HEADS,), 0.5)
    ln_v_g = 1.0 + nrm(ks[4], (GMLP_WIDTH,), 0.05)
    ln_v_b = nrm(ks[5], (GMLP_WIDTH,), 0.02)
    w_spatial = nrm(ks[6], (N_GMLP_GROUPS, CHUNK, CHUNK), CHUNK ** -0.5)
    b_spatial = 1.0 + nrm(ks[7], (N_GMLP_GROUPS, CHUNK), 0.05)
    w_out = nrm(ks[8], (MIX_WIDTH_2, D_MODEL), MIX_WIDTH_2 ** -0.5 * DEEPNORM_BETA_2)
    b_out = nrm(ks[9], (D_MODEL,), 0.02)
    ln1_g = 1.0 + nrm(ks[10], (D_MODEL,), 0.05)
    ln1_b = nrm(ks[11], (D_MODEL,), 0.02)
    w_router = nrm(ks[12], (D_MODEL, N_EXPERTS), D_MODEL ** -0.5)
    b_router = nrm(ks[13], (N_EXPERTS,), 0.01)
    w_gate = nrm(ks[14], (N_EXPERTS, D_MODEL, D_FF_2), D_MODEL ** -0.5)
    b_gate = nrm(ks[15], (N_EXPERTS, D_FF_2), 0.02)
    w_up = nrm(ks[16], (N_EXPERTS, D_MODEL, D_FF_2), D_MODEL ** -0.5 * DEEPNORM_BETA_2)
    b_up = nrm(ks[17], (N_EXPERTS, D_FF_2), 0.02)
    w_down = nrm(ks[18], (N_EXPERTS, D_FF_2, D_MODEL), D_FF_2 ** -0.5 * DEEPNORM_BETA_2)
    b_down = nrm(ks[19], (N_EXPERTS, D_MODEL), 0.02)
    ln2_g = 1.0 + nrm(ks[20], (D_MODEL,), 0.05)
    ln2_b = nrm(ks[21], (D_MODEL,), 0.02)
    return {"x": x, "w_in": w_in, "b_in": b_in, "sinks": sinks, "ln_v_g": ln_v_g, "ln_v_b": ln_v_b,
            "w_spatial": w_spatial, "b_spatial": b_spatial, "w_out": w_out, "b_out": b_out,
            "ln1_g": ln1_g, "ln1_b": ln1_b, "w_router": w_router, "b_router": b_router,
            "w_gate": w_gate, "b_gate": b_gate, "w_up": w_up, "b_up": b_up,
            "w_down": w_down, "b_down": b_down, "ln2_g": ln2_g, "ln2_b": ln2_b}

def second_block(x, w_in, b_in, sinks, ln_v_g, ln_v_b, w_spatial, b_spatial, w_out, b_out,
              ln1_g, ln1_b, w_router, b_router, w_gate, b_gate, w_up, b_up,
              w_down, b_down, ln2_g, ln2_b):
    for l in range(DEPTH):
        mix = token_mixer(x, w_in[l], b_in[l], sinks[l], ln_v_g[l], ln_v_b[l],
                          w_spatial[l], b_spatial[l], w_out[l], b_out[l])
        h = layer_norm_2(DEEPNORM_ALPHA_2 * x + mix, ln1_g[l], ln1_b[l])
        ffn = routed_experts(h, w_router[l], b_router[l], w_gate[l], b_gate[l],
                             w_up[l], b_up[l], w_down[l], b_down[l])
        x = layer_norm_2(DEEPNORM_ALPHA_2 * h + ffn, ln2_g[l], ln2_b[l])
    return x


def setup_inputs(seed=0):
    out = dict(first_inputs(seed))
    for name, value in second_inputs(seed + 1).items():
        if name != "x":
            out[name + "_2"] = value
    return out


def reference(
    x, c, w_ada, b_ada, w_in, conv_w, conv_b, dt_bias, a_log, d_skip, ssm_norm_w, f_bias,
    attn_norm_w, w_out, ln1_g, ln1_b, w_ff_in, w_ff_out, ln2_g, ln2_b, w_in_2, b_in_2, sinks_2,
    ln_v_g_2, ln_v_b_2, w_spatial_2, b_spatial_2, w_out_2, b_out_2, ln1_g_2, ln1_b_2,
    w_router_2, b_router_2, w_gate_2, b_gate_2, w_up_2, b_up_2, w_down_2, b_down_2, ln2_g_2,
    ln2_b_2,
):
    x = first_block(
        x, c, w_ada, b_ada, w_in, conv_w, conv_b, dt_bias, a_log, d_skip, ssm_norm_w, f_bias,
        attn_norm_w, w_out, ln1_g, ln1_b, w_ff_in, w_ff_out, ln2_g, ln2_b,
    )
    return second_block(
        x, w_in_2, b_in_2, sinks_2, ln_v_g_2, ln_v_b_2, w_spatial_2, b_spatial_2, w_out_2,
        b_out_2, ln1_g_2, ln1_b_2, w_router_2, b_router_2, w_gate_2, b_gate_2, w_up_2, b_up_2,
        w_down_2, b_down_2, ln2_g_2, ln2_b_2,
    )


_drawn_inputs = setup_inputs


def setup_inputs(seed=0):
    import zlib

    import numpy as np

    out = dict(_drawn_inputs(seed))
    spreads = {}
    factors = {'conv_b': 6.241,
     'ln1_b': 2.981,
     'ln2_b': 3.117,
     'b_in_2': 3.012,
     'sinks_2': 50.595,
     'ln_v_g_2': 5.92,
     'ln_v_b_2': 25.869,
     'b_spatial_2': 4.199,
     'b_router_2': 3.664,
     'b_gate_2': 8.0,
     'b_up_2': 8.0,
     'b_down_2': 6.376,
     'ln2_b_2': 2.851,
     'b_out_2': 2.905}
    for name, (base, spread) in spreads.items():
        noise = np.random.default_rng([zlib.crc32(name.encode()), seed]).standard_normal(out[name].shape)
        drawn = base * np.exp(spread * noise) if base else spread * noise
        out[name] = __import__('jax').numpy.asarray(drawn.astype(out[name].dtype))
    for name, factor in factors.items():
        out[name] = (out[name] * factor).astype(out[name].dtype)
    return out
```

```python
from contextlib import ExitStack

import concourse.bass as bass
from concourse import mybir

F32 = mybir.dt.float32
BF16 = mybir.dt.bfloat16
I32 = mybir.dt.int32
U32 = mybir.dt.uint32
ALU = mybir.AluOpType
ACT = mybir.ActivationFunctionType
AX_X = mybir.AxisListType.X

P = 128
D = 1024
S = 512
T = S // P
KB = D // P
HALF = 512
SSM_HEADS = 16
HEAD = 64
CONV_DIM = 1536
CONV_W = 4
XB = CONV_DIM // P
ATT_HEADS = 16
D_FF = 4096
FG = D_FF // D
Q_HEADS = 8
WIN_COLS = 5664
C_Z, C_XBC, C_DT, C_Q, C_F = 0, 1024, 2560, 2576, 5648
ALPHA = 2.0 ** 0.25
EPS = 1e-5
NEG = -1e30
EXPERTS = 32
TOP_K = 4
CAP = 128
MAX_SLOTS = S * TOP_K // CAP + EXPERTS - 1
LIST = MAX_SLOTS + 1

SLOT = 4096
RING = 4


class Shared:
    pass


def rows_of(w, r0, nb, c0, nc_):
    return w[r0:r0 + nb * P, c0:c0 + nc_].rearrange("(k p) n -> p k n", p=P)


def plan_weights(A):
    w_ada, w_in, w_out = A["w_ada"][0], A["w_in"][0], A["w_out"][0]
    plan = []
    for q in range(4):
        plan.append((("ada1", q), 2048, [(0, 2 * 2048, rows_of(w_ada, 2 * q * P, 2, 0, 2048))]))
    cols = [("xbc", 0), ("xbc", 1), ("xbc", 2), ("z", 0), ("z", 1)]
    gates = 0
    for kind, n in cols:
        c0 = (C_XBC if kind == "xbc" else C_Z) + HALF * n
        plan.append(((kind, n), HALF, [(0, KB * HALF, rows_of(w_in, 0, KB, c0, HALF))]))
        for _ in range(2 if gates < KB else 0):
            plan.append((("ada2", gates), 4096, [(0, 4096, rows_of(w_ada, gates * P, 1, 2048, 4096))]))
            gates += 1
    for j in range(ATT_HEADS // 2):
        plan.append((("qkv", j), P, [(m * KB * P, KB * P, rows_of(w_in, 0, KB, C_Q + m * D + j * P, P))
                                     for m in range(3)]))
    for q in range(4):
        plan.append((("out", q), D, [(0, SLOT, rows_of(w_out, q * HALF, 4, 0, D))]))
    for g, kind in ((0, 0), (1, 0), (0, 1), (2, 0), (1, 1), (3, 0), (2, 1), (3, 1)):
        for h in range(2 if kind == 0 else 0):
            plan.append((("up", g, h), HALF, [(0, SLOT, rows_of(A["w_ff_in"][0], 0, KB, g * D + h * HALF, HALF))]))
        for h in range(2 if kind == 1 else 0):
            plan.append((("down", g, h), D, [(0, SLOT, rows_of(A["w_ff_out"][0], g * D + h * HALF, 4, 0, D))]))
    w2 = A["w_in_2"][0]
    plan.append((("q2",), HALF, [(0, SLOT, rows_of(w2, 0, KB, 0, HALF))]))
    plan.append((("kv2",), 2 * P, [(0, KB * 2 * P, rows_of(w2, 0, KB, HALF, 2 * P))]))
    plan.append((("u2",), HALF, [(0, SLOT, rows_of(w2, 0, KB, 768, HALF))]))
    plan.append((("g2",), HALF, [(0, SLOT, rows_of(w2, 0, KB, 1280, HALF))]))
    for q in range(2):
        plan.append((("out2", q), D, [(0, SLOT, rows_of(A["w_out_2"][0], q * HALF, 4, 0, D))]))
    return plan


class Weights:

    def __init__(self, nc, ctx, A):
        self.plan = plan_weights(A)
        self.index = {c[0]: n for n, c in enumerate(self.plan)}
        self.ring = ctx.enter_context(nc.sbuf_tensor("weight_ring", [P, RING * SLOT], F32))
        self.landed = [ctx.enter_context(nc.semaphore(f"weights_landed{i}")) for i in range(RING)]
        self.used = ctx.enter_context(nc.semaphore("weights_used"))
        self.value, count = [], [0] * RING
        for n, (_, _, parts) in enumerate(self.plan):
            count[n % RING] += 16 * len(parts)
            self.value.append(count[n % RING])
        self.final = count

    def view(self, key):
        n = self.index[key]
        row = self.plan[n][1]
        size = sum(x[1] for x in self.plan[n][2])
        at = (n % RING) * SLOT
        return self.ring[:, at:at + size].rearrange("p (k n) -> p k n", n=row)

    def wait(self, pe, key):
        n = self.index[key]
        pe.wait_ge(self.landed[n % RING], self.value[n])

    def load(self, sp, keys):
        for key in keys:
            n = self.index[key]
            if n >= RING:
                sp.wait_ge(self.used, n - RING + 1)
            at = (n % RING) * SLOT
            for off, size, src in self.plan[n][2]:
                dst = self.ring[:, at + off:at + off + size].rearrange("p (k n) -> p k n", n=src.shape[-1])
                sp.dma_start(dst, src).then_inc(self.landed[n % RING], 16)

    def upto(self, sp, stop):
        keys = [c[0] for c in self.plan[self.sent:stop]]
        self.sent = max(self.sent, stop)
        self.load(sp, keys)

    sent = 0


def chain(eng, sem):
    count = [0]

    def step(ins):
        count[0] += 1
        ins.then_inc(sem, 1)
        eng.wait_ge(sem, count[0])
    return step


def bc_mid(ap, n):
    return ap.unsqueeze(1).to_broadcast([ap.shape[0], n, ap.shape[-1]])


def bc_last(ap, n):
    return ap.unsqueeze(2).to_broadcast([ap.shape[0], ap.shape[-1], n])


R_C, R_SSMW, R_ATTW, R_CB, R_CW = 0, 8, 16, 24, 36
R_SH1, R_SC1, R_SH2, R_SC2, R_B2 = 84, 92, 100, 108, 116
R_ALL = 121


def stage_prepare(nc, A, G):
    with ExitStack() as ctx:
        def sb(name, shape, dt=F32):
            return ctx.enter_context(nc.sbuf_tensor(name, shape, dt))

        sem = G.sem

        prow = sb("param_rows", [R_ALL, P])
        x_tok = sb("x_tok", [P, T, D])
        mod_rows = sb("mod_rows", [P, HALF])
        mod_col = sb("mod_col", [P, 2 * KB])
        params_in, x_in, consts, ident_ok = sem("params_in"), sem("x_in"), sem("consts"), sem("ident_ok")
        pcol_t, pcol_ok, cact_ok = sem("pcol_t"), sem("pcol_ok"), sem("cact_ok")
        rows_ok, cols_done, mod_ok = sem("rows_ok"), sem("cols_done"), sem("mod_ok")
        xt_done, h_ok, dsk_ok = sem("x_transposed"), sem("h_ok"), sem("dsk_ok")
        dsk2 = sb("d_skip_pairs", [2, KB])
        halves = sb("halves", [2, P])
        ps = G.ps
        b_ada = A["b_ada"][0].rearrange("(r n) -> r n", n=P)
        block = ctx.enter_context(nc.Block())

        @block.sync
        def _(sp):
            G.W.upto(sp, RING + 4)

        @block.gpsimd
        def _(pool):
            nc.gpsimd.memset(G.ident[:], 0.0).then_inc(consts, 1)
            nc.gpsimd.memset(G.tri[:], 1.0).then_inc(consts, 1)
            nc.gpsimd.memset(G.strict[:], 1.0).then_inc(consts, 1)
            nc.gpsimd.memset(G.ones[:], 1.0).then_inc(consts, 1)
            nc.gpsimd.memset(G.late[:], 0.0).then_inc(consts, 1)
            nc.gpsimd.memset(G.ident_bf[:], 0.0).then_inc(consts, 1)
            nc.gpsimd.memset(G.causal_bf[:], 0.0).then_inc(consts, 1)
            nc.gpsimd.memset(G.before_bf[:], 0.0).then_inc(consts, 1)
            nc.gpsimd.memset(halves[:], 1.0).then_inc(consts, 1)
            pool.wait_ge(consts, 9)

            def keep(tile, op, base, step, mult, fill):
                return nc.gpsimd.affine_select(out=tile[:], in_=tile[:], compare_op=op, fill=fill, base=base,
                                               pattern=[[step, P]], channel_multiplier=mult)
            keep(G.ident, ALU.not_equal, 0, -1, 1, 1.0).then_inc(ident_ok, 1)
            keep(G.ident_bf, ALU.not_equal, 0, -1, 1, 1.0).then_inc(ident_ok, 1)
            keep(G.tri, ALU.is_ge, 0, 1, -1, 0.0).then_inc(ident_ok, 1)
            keep(G.strict, ALU.is_gt, 0, 1, -1, 0.0).then_inc(ident_ok, 1)
            keep(G.late, ALU.is_ge, 0, 1, -1, NEG).then_inc(ident_ok, 1)
            keep(G.causal_bf, ALU.is_ge, 0, -1, 1, NEG).then_inc(ident_ok, 1)
            keep(G.before_bf, ALU.is_gt, 0, 1, -1, NEG).then_inc(ident_ok, 1)
            keep(halves, ALU.is_ge, 0, 1, -HEAD, 0.0).then_inc(consts, 1)
            pool.wait_ge(consts, 10)
            keep(halves, ALU.is_ge, HEAD - 1, -1, HEAD, 0.0).then_inc(ident_ok, 1)

        @block.scalar
        def _(act):
            parts = [
                (R_C, A["c"].rearrange("a (r n) -> (a r) n", n=P)),
                (R_SSMW, A["ssm_norm_w"][0].rearrange("(r n) -> r n", n=P)),
                (R_ATTW, A["attn_norm_w"][0].rearrange("(r n) -> r n", n=P)),
                (R_CB, A["conv_b"][0].rearrange("(r n) -> r n", n=P)),
                (R_CW, A["conv_w"][0].rearrange("w (r n) -> (w r) n", n=P)),
                (R_SH1, b_ada[0:16, :]),
                (R_SH2, b_ada[24:40, :]),
                (R_B2 + 4, A["b_in_2"][0:1, HALF:HALF + P]),
            ]
            for r, src in parts:
                act.dma_start(prow[r:r + src.shape[0], :], src).then_inc(params_in, 16)
            for a in range(2):
                act.dma_start(prow[R_B2:R_B2 + 4, a * HEAD:(a + 1) * HEAD],
                              A["b_in_2"][0][a * 256:(a + 1) * 256].rearrange("(j n) -> j n", n=HEAD))\
                   .then_inc(params_in, 16)
            for t in range(T):
                act.dma_start(x_tok[:, t, :], A["x"][0, t * P:(t + 1) * P, :]).then_inc(x_in, 16)
            with nc.allow_non_contiguous_dma(reason="sixteen numbers"):
                act.dma_start(dsk2[:], A["d_skip"][0].rearrange("(j a) -> a j", a=2)).then_inc(params_in, 16)
            wi = A["w_in"][0]
            act.dma_start(G.w_dtf[:, :, 0:16], rows_of(wi, 0, KB, C_DT, 16)).then_inc(G.dtf_in, 16)
            act.dma_start(G.w_dtf[:, :, 16:32], rows_of(wi, 0, KB, C_F, 16)).then_inc(G.dtf_in, 16)
            for n, name in enumerate(("dt_bias", "f_bias", "a_log")):
                act.dma_start(G.head_rows[:, 16 * n:16 * n + 16],
                              A[name][0:1, :].to_broadcast([P, 16])).then_inc(G.dtf_in, 16)
            act.wait_ge(pcol_ok, 1)
            nc.scalar.activation(G.c_act[:], G.pcol[:, R_C:R_C + KB], ACT.Silu).then_inc(cact_ok, 1)
            act.wait_ge(dsk_ok, 1)
            nc.scalar.copy(G.d_col[:], ps[:, 1, 0:KB]).then_inc(dsk_ok, 1)
            act.wait_ge(G.W.used, 4)
            for j in range(2, 4):
                nc.scalar.copy(mod_rows[32 * j:32 * j + 1, :], ps[32 * j:32 * j + 1, 2, :]).then_inc(rows_ok, 1)

        @block.tensor
        def _(pe):
            pe.wait_ge(params_in, 16 * 11)
            pe.wait_ge(ident_ok, 8)
            nc.tensor.transpose(ps[:, 0, 0:R_ALL], prow[:], G.ident[0:R_ALL, 0:R_ALL]).then_inc(pcol_t, 1)
            nc.tensor.matmul(ps[:, 1, 0:KB], halves[:], dsk2[:], start=True, stop=True).then_inc(dsk_ok, 1)
            pe.wait_ge(x_in, 16 * T)

            def transpose_x(k):
                if k >= 4:
                    pe.wait_ge(h_ok, k - 3)
                for t in range(T):
                    m = nc.tensor.transpose(ps[:, 4 + k % 4, t * P:(t + 1) * P], x_tok[:, t, k * P:(k + 1) * P],
                                            G.ident[:])
                m.then_inc(xt_done, 1)
            for k in range(4):
                transpose_x(k)
            pe.wait_ge(cact_ok, 1)
            for k in range(KB):
                G.W.wait(pe, ("ada1", k // 2))
                w = G.W.view(("ada1", k // 2))
                for j in range(4):
                    m = nc.tensor.matmul(ps[32 * j:32 * j + 1, 2, :], G.c_act[:, k:k + 1],
                                         w[:, k % 2, j * HALF:(j + 1) * HALF], start=(k == 0), stop=(k == KB - 1))
                if k % 2:
                    m.then_inc(G.W.used, 1)
            pe.wait_ge(rows_ok, 4)
            pe.wait_ge(dsk_ok, 2)
            for n in range(16):
                j, seg = n // 4, n % 4
                m = nc.tensor.matmul(ps[:, j, n:n + 1], mod_rows[32 * j:32 * j + 1, seg * P:(seg + 1) * P],
                                     G.ones[32 * j:32 * j + 1, 0:1], start=True, stop=True)
            m.then_inc(cols_done, 1)
            for k in range(4, KB):
                transpose_x(k)

        @block.vector
        def _(dve):
            dve.wait_ge(pcol_t, 1)
            nc.vector.tensor_copy(G.pcol[:, 0:R_ALL], ps[:, 0, 0:R_ALL]).then_inc(pcol_ok, 1)
            dve.wait_ge(G.W.used, 4)
            for j in range(2):
                nc.vector.tensor_copy(mod_rows[32 * j:32 * j + 1, :], ps[32 * j:32 * j + 1, 2, :]).then_inc(rows_ok, 1)
            dve.wait_ge(cols_done, 1)
            for j in range(4):
                at = slice(4 * j, 4 * j + 4)
                nc.vector.scalar_tensor_tensor(out=mod_col[:, at], in0=ps[:, j, at], scalar=float(j // 2),
                                               in1=G.pcol[:, R_SH1 + 4 * j:R_SH1 + 4 * j + 4], op0=ALU.add,
                                               op1=ALU.add).then_inc(mod_ok, 1)
            dve.wait_ge(mod_ok, 4)
            for k in range(KB):
                dve.wait_ge(xt_done, k + 1)
                nc.vector.tensor_scalar(G.hT[:, k, :], ps[:, 4 + k % 4, :], mod_col[:, KB + k:KB + k + 1],
                                        mod_col[:, k:k + 1], ALU.mult, ALU.add).then_inc(h_ok, 1)

def stage_streams(nc, A, G):
    with ExitStack() as ctx:
        def sb(name, shape, dt=F32):
            return ctx.enter_context(nc.sbuf_tensor(name, shape, dt))

        sem = G.sem

        ps = G.ps
        PAD = CONV_W - 1
        raw = sb("conv_in", [P, 3, PAD + S])
        acc = sb("conv_acc", [P, 2, S])
        v = sb("dtf", [P, T, 32])
        mag = sb("dtf_mag", [P, T, 32])
        e = sb("dtf_exp", [P, T, 32])
        u = sb("dtf_u", [P, T, 32])
        lnu = sb("dtf_ln", [P, T, 32])
        r = sb("dtf_r", [P, T, 32])
        sign = sb("sign_row", [P, 32])
        mul = sb("rate_row", [P, 32])
        rows = sb("sum_rows", [48, S])
        gates = sb("gate_rows", [P, 2, HALF])
        bg = sb("gate_bias", [P, 2, D])
        f_done, f_read, conv_acc, conv_free = sem("f_done"), sem("f_read"), sem("conv_acc_ok"), sem("conv_free")
        pads, dtf_done, dtf_ok, mag_ok, e_ok, u_ok, ln_ok = (sem(x) for x in (
            "pads", "dtf_done", "dtf_step", "mag_ok", "e_ok", "u_ok", "ln_ok"))
        conv_step, rate_ok, av_ok, sums_done, sums_ok = (sem(x) for x in (
            "conv_step", "rate_ok", "av_ok", "sums_done", "sums_ok"))
        diff_ok, rows_ok, g_rows, g_all, gcols, gstep = (sem(x) for x in (
            "diff_ok", "rows_ready", "g_rows", "g_all", "gcols", "gstep"))
        acc_free = sem("acc_free")
        gates_done = sem("gates_done")
        FB = XB + KB
        block = ctx.enter_context(nc.Block())

        @block.sync
        def _(sp):
            G.W.upto(sp, G.W.index[("qkv", 0)] + RING)
            sp.wait_ge(rows_ok, 2)
            sp.dma_start(G.sums_dram[0:16, :], rows[0:16, :]).then_inc(G.sums_out, 16)
            sp.dma_start(G.sums_dram[16:32, :], rows[32:48, :]).then_inc(G.sums_out, 16)

        @block.gpsimd
        def _(pool):
            nc.gpsimd.memset(raw[:, :, 0:PAD], 0.0).then_inc(pads, 1)
            nc.gpsimd.memset(sign[:, 0:16], 1.0).then_inc(pads, 1)
            nc.gpsimd.memset(sign[:, 16:32], -1.0).then_inc(pads, 1)
            nc.gpsimd.memset(mul[:, 16:32], -1.0).then_inc(pads, 1)
            for m, c0 in ((0, 2 * D), (1, 5 * D)):
                pool.dma_start(bg[:, m, :], A["b_ada"][0:1, c0:c0 + D].to_broadcast([P, D])).then_inc(G.gate_bias_in, 16)
            pool.wait_ge(g_rows, 8)
            for m in range(2):
                for h in range(2):
                    q = 64 * m + 32 * h
                    nc.gpsimd.partition_broadcast(G.gate[:, m, h * HALF:(h + 1) * HALF],
                                                  gates[q:q + 1, m, :]).then_inc(g_all, 1)
            pool.wait_ge(G.gate_bias_in, 32)
            pool.wait_ge(g_all, 4)
            nc.gpsimd.tensor_tensor(G.gate[:], G.gate[:], bg[:], ALU.add).then_inc(g_all, 1)
            pool.wait_ge(g_all, 5)
            nc.gpsimd.tensor_scalar(G.gate[:], G.gate[:], 1.0, None, ALU.add).then_inc(g_all, 1)

        @block.scalar
        def _(act):
            act.wait_ge(G.dtf_in, 16 * 5)
            nc.scalar.activation(mul[:, 0:16], G.head_rows[:, 32:48], ACT.Exp).then_inc(rate_ok, 1)
            act.wait_ge(mag_ok, 1)
            nc.scalar.activation(e[:], mag[:], ACT.Exp, scale=-1.0).then_inc(e_ok, 1)
            act.wait_ge(u_ok, 1)
            nc.scalar.activation(lnu[:], u[:], ACT.Ln).then_inc(ln_ok, 1)

            def silu_conv(n):
                act.wait_ge(conv_acc, n + 1)
                nc.scalar.activation(G.xbcT[:, n, :], acc[:, n % 2, :], ACT.Silu,
                                     bias=G.pcol[:, R_CB + n:R_CB + n + 1]).then_inc(acc_free, 1)

            act.wait_ge(pads, 1)
            for n in range(FB):
                if n == 6:
                    act.wait_ge(diff_ok, 1)
                    nc.scalar.activation(G.decays[:], G.decays[:], ACT.Exp).then_inc(G.decays_ok, 1)
                act.wait_ge(f_done, n + 1)
                if n < XB:
                    if n >= 3:
                        act.wait_ge(conv_acc, n - 2)
                    nc.scalar.copy(raw[:, n % 3, PAD:], ps[:, n % 4, :]).then_inc(f_read, 1)
                else:
                    nc.scalar.activation(G.mixT[:, n - XB, :], ps[:, n % 4, :], ACT.Silu).then_inc(f_read, 1)
                if 1 <= n <= XB:
                    silu_conv(n - 1)

        @block.tensor
        def _(pe):
            pe.wait_ge(G.dtf_in, 16 * 5)
            for t in range(T):
                for k in range(KB):
                    m = nc.tensor.matmul(ps[:, 7, t * 32:t * 32 + 32], G.hT[:, k, t * P:(t + 1) * P],
                                         G.w_dtf[:, k, :], start=(k == 0), stop=(k == KB - 1))
            m.then_inc(dtf_done, 1)

            def gate_chunk(k):
                G.W.wait(pe, ("ada2", k))
                w = G.W.view(("ada2", k))
                for b in range(2):
                    for j in range(4):
                        c0 = b * 2048 + j * HALF
                        m = nc.tensor.matmul(ps[32 * j:32 * j + 1, 4 + b, :], G.c_act[:, k:k + 1], w[:, 0, c0:c0 + HALF],
                                             start=(k == 0), stop=(k == KB - 1))
                m.then_inc(G.W.used, 1)

            def sums():
                pe.wait_ge(av_ok, 1)
                for t in range(T):
                    nc.tensor.matmul(ps[:, 6, 64 + 16 * t:80 + 16 * t], G.tri[:], G.av[:, t, 0:16], start=True, stop=True)
                    nc.tensor.matmul(ps[:, 6, 16 * t:16 * t + 16], G.ones[:], G.av[:, t, 0:16], start=True, stop=True)
                for t in range(T):
                    at = slice(t * P, (t + 1) * P)
                    nc.tensor.matmul(ps[0:16, 7, at], G.av[:, t, 0:16], G.tri[:], start=True, stop=True)
                    for b in range(t):
                        nc.tensor.matmul(ps[32:48, 7, at], G.av[:, b, 16:32], G.ones[:], start=(b == 0), stop=False)
                    m = nc.tensor.matmul(ps[32:48, 7, at], G.av[:, t, 16:32], G.tri[:], start=(t == 0), stop=True)
                m.then_inc(sums_done, 1)

            n = 0
            for c, key in enumerate([("xbc", 0), ("xbc", 1), ("xbc", 2), ("z", 0), ("z", 1)]):
                G.W.wait(pe, key)
                w = G.W.view(key)
                for b in range(4):
                    if n >= 4:
                        pe.wait_ge(f_read, n - 3)
                    for k in range(KB):
                        m = nc.tensor.matmul(ps[:, n % 4, :], w[:, k, b * P:(b + 1) * P], G.hT[:, k, :],
                                             start=(k == 0), stop=(k == KB - 1))
                    m.then_inc(f_done, 1)
                    n += 1
                    if n == 3:
                        sums()
                pe.wait_ge(f_done, n)
                nc.tensor.nop().then_inc(G.W.used, 1)
                if c < 4:
                    gate_chunk(2 * c)
                    gate_chunk(2 * c + 1)
            pe.wait_ge(g_rows, 8)
            for i in range(16):
                b, h, seg = i // 8, (i % 8) // 4, i % 4
                q = (64 if b == 0 else 0) + 32 * h
                m = nc.tensor.matmul(ps[:, 4 + (q // 32 + 2) % 4, 128 + i:129 + i], gates[q:q + 1, b, seg * P:(seg + 1) * P],
                                     G.ones[q:q + 1, 0:1], start=True, stop=True)
            m.then_inc(gcols, 1)

        @block.vector
        def _(dve):
            step = chain(dve, dtf_ok)
            dve.wait_ge(dtf_done, 1)
            dve.wait_ge(pads, 4)
            step(nc.vector.tensor_tensor(v[:], ps[:, 7, 0:T * 32].rearrange("p (t h) -> p t h", h=32),
                                         bc_mid(G.head_rows[:, 0:32], T), ALU.add))
            step(nc.vector.tensor_tensor(v[:], v[:], bc_mid(sign[:], T), ALU.mult))
            nc.vector.scalar_tensor_tensor(out=mag[:], in0=v[:], scalar=-1.0, in1=v[:], op0=ALU.mult, op1=ALU.max).then_inc(mag_ok, 1)
            dve.wait_ge(e_ok, 1)
            nc.vector.tensor_scalar(u[:], e[:], 1.0, None, ALU.add).then_inc(u_ok, 1)
            dve.wait_ge(u_ok, 1)
            step(nc.vector.reciprocal(r[:], u[:]))
            step(nc.vector.scalar_tensor_tensor(out=mag[:], in0=u[:], scalar=-1.0, in1=e[:], op0=ALU.add,
                                                op1=ALU.subtract))
            step(nc.vector.tensor_tensor(r[:], r[:], mag[:], ALU.mult))
            dve.wait_ge(ln_ok, 1)
            step(nc.vector.tensor_tensor(r[:], lnu[:], r[:], ALU.subtract))
            step(nc.vector.scalar_tensor_tensor(out=v[:], in0=v[:], scalar=0.0, in1=r[:], op0=ALU.max, op1=ALU.add))
            dve.wait_ge(rate_ok, 1)
            step(nc.vector.tensor_scalar(mul[:, 0:16], mul[:, 0:16], -1.0, None, ALU.mult))
            step(nc.vector.tensor_copy(G.dt[:], v[:, :, 0:16]))
            nc.vector.tensor_tensor(G.av[:], v[:], bc_mid(mul[:], T), ALU.mult).then_inc(av_ok, 1)

            def sums():
                dve.wait_ge(sums_done, 1)
                nc.vector.tensor_copy(rows[0:16, :], ps[0:16, 7, :]).then_inc(rows_ok, 1)
                nc.vector.tensor_scalar(rows[32:48, :], ps[32:48, 7, :], -1.0, None, ALU.mult).then_inc(rows_ok, 1)
                step(nc.vector.tensor_copy(G.acs[:], ps[:, 6, 64:128]))
                step(nc.vector.tensor_copy(G.decays[:, 0:64], ps[:, 6, 0:64]))
                nc.vector.tensor_tensor(G.decays[:, 64:128], G.decays[:, 0:64], G.acs[:], ALU.subtract).then_inc(diff_ok, 1)

            cstep = chain(dve, conv_step)
            for n in range(XB):
                dve.wait_ge(f_read, n + 1)
                if n >= 2:
                    dve.wait_ge(acc_free, n - 1)
                w = G.pcol[:, R_CW:R_CW + CONV_W * XB].rearrange("p (w n) -> p w n", n=XB)
                a = acc[:, n % 2, :]
                cstep(nc.vector.tensor_scalar(a, raw[:, n % 3, 0:S], w[:, 0, n:n + 1], None, ALU.mult))
                for i in range(1, CONV_W):
                    m = nc.vector.scalar_tensor_tensor(out=a, in0=raw[:, n % 3, i:i + S], scalar=w[:, i, n:n + 1],
                                                       in1=a, op0=ALU.mult, op1=ALU.add)
                    cstep(m) if i < CONV_W - 1 else m.then_inc(conv_acc, 1)
                if n == 3:
                    sums()
            dve.wait_ge(G.W.used, G.W.index[("ada2", KB - 1)] + 1)
            for b in range(2):
                for j in range(4):
                    nc.vector.tensor_copy(gates[32 * j:32 * j + 1, b, :], ps[32 * j:32 * j + 1, 4 + b, :]).then_inc(g_rows, 1)
            dve.wait_ge(gcols, 1)
            for i in range(4):
                at = slice(4 * i, 4 * i + 4)
                nc.vector.scalar_tensor_tensor(out=G.mod2[:, at], in0=ps[:, 4 + i, 128 + 4 * i:132 + 4 * i],
                                               scalar=float(i // 2), in1=G.pcol[:, R_SH2 + 4 * i:R_SH2 + 4 * i + 4],
                                               op0=ALU.add, op1=ALU.add).then_inc(gstep, 1)


def stage_mixer(nc, A, G):
    PAIRS = ATT_HEADS // 2
    STEPS = T * 2
    UNITS = T * 2
    FROM = [P * (b * T - b * (b - 1) // 2) for b in range(T)]
    with ExitStack() as ctx:
        def sb(name, shape, dt=F32):
            return ctx.enter_context(nc.sbuf_tensor(name, shape, dt))

        sem = G.sem

        ps = G.ps
        B_PROJ, B_LOG, B_TR, B_X, B_Y, B_PV = 0, 2, 4, 5, 6, 7
        qT = sb("qT", [P, 2, S])
        kT = sb("kT", [P, 2, S])
        vv = sb("v_tok", [P, 2, T, P])
        nb = sb("key_bias", [P, 2, S])
        lg = sb("probs", [P, 4, S])
        pT = sb("probs_T", [P, 2, T * (T + 1) // 2 * P])
        st = sb("att_stats", [P, 3, 4])
        acsb = sb("acs_rows", [P, 8, P])
        dm = sb("decay", [P, 8, P])
        ctd = sb("c_decayed", [P, 8, P])
        xc = sb("x_dt", [P, 8, HEAD])
        xcd = sb("x_dt_end", [P, 8, HEAD])
        bt = sb("b_tok", [P, P])
        state = sb("state", [P, 2, 8, HEAD])
        ytmp = sb("y_tmp", [P, 4, P])
        names = ("proj_done proj_read logits_done logits_read max_ready exp_done rinv_ready probs_ready pt_done "
                 "pt_copied pv_done pv_read xt_done bcb_done xc_ready xcd_ready bt_ready dm_sub dm_masked decay_ready "
                 "eacs_ready sc_ready ctd_ready y_done y_read ssm_out s_done state_ready state_step").split()
        q = {x: sem(x) for x in names}
        nb_in = sem("nb_in")
        acs_in = sem("acs_in")
        block = ctx.enter_context(nc.Block())

        @block.sync
        def _(sp):
            sp.wait_ge(G.sums_out, 32)
            for j in range(PAIRS):
                c, g = j // 2, j % 2
                if j:
                    sp.wait_ge(q["dm_sub"], j)
                    sp.wait_ge(q["eacs_ready"], j)
                sp.dma_start(acsb[:], G.sums_dram[8 * g:8 * g + 8, c * P:(c + 1) * P].unsqueeze(0)
                             .to_broadcast([P, 8, P])).then_inc(acs_in, 16)
                if j:
                    sp.wait_ge(q["logits_read"], UNITS * j)
                sp.dma_start(nb[:], G.sums_dram[16 + 2 * j:18 + 2 * j, :].unsqueeze(0)
                             .to_broadcast([P, 2, S])).then_inc(nb_in, 16)
                G.W.upto(sp, G.W.index[("qkv", 0)] + RING + j + 1)

        @block.gpsimd
        def _(pool):
            def scale_probs(U):
                i = (U % UNITS) // 2
                n = (i + 1) * P
                pool.wait_ge(q["rinv_ready"], U + 1)
                nc.gpsimd.tensor_scalar(lg[:, U % 4, 0:n], lg[:, U % 4, 0:n], st[:, 2, U % 4:U % 4 + 1], None,
                                        ALU.mult).then_inc(q["probs_ready"], 1)

            def ssm(n):
                c, g = n // 2, n % 2
                pool.wait_ge(q["xc_ready"], n + 1)
                pool.wait_ge(G.decays_ok, 1)
                if n:
                    pool.wait_ge(q["s_done"], n)
                nc.gpsimd.tensor_tensor(xcd[:], xc[:],
                                        bc_last(G.decays[:, 64 + 16 * c + 8 * g:72 + 16 * c + 8 * g], HEAD),
                                        ALU.mult).then_inc(q["xcd_ready"], 1)
                pool.wait_ge(q["dm_sub"], n + 1)
                nc.gpsimd.tensor_tensor(dm[:], dm[:], bc_mid(G.late[:], 8), ALU.add)\
                    .then_inc(q["dm_masked"], 1)
                pool.wait_ge(q["eacs_ready"], n + 1)
                nc.gpsimd.tensor_tensor(ctd[:], ctd[:],
                                        bc_mid(G.xbcT[:, 10 + g, c * P:(c + 1) * P], 8), ALU.mult)\
                    .then_inc(q["ctd_ready"], 1)
            for j in range(PAIRS + 1):
                if j < PAIRS:
                    ssm(j)
                if j >= 1:
                    for u in range(UNITS):
                        scale_probs((j - 1) * UNITS + u)

        @block.scalar
        def _(act):
            def proj(j, m):
                n = 3 * j + m
                act.wait_ge(q["proj_done"], n + 1)
                if j >= 2:
                    act.wait_ge(q["pv_done"], j - 1)
                src = ps[:, B_PROJ + n % 2, :]
                if m == 0:
                    ins = nc.scalar.mul(qT[:, j % 2, :], src, HEAD ** -0.5)
                elif m == 1:
                    ins = nc.scalar.copy(kT[:, j % 2, :], src)
                else:
                    ins = nc.scalar.copy(vv[:, j % 2].rearrange("p t n -> p (t n)"), src)
                ins.then_inc(q["proj_read"], 1)

            def exps(U):
                i = (U % UNITS) // 2
                n = (i + 1) * P
                act.wait_ge(q["max_ready"], U + 1)
                nc.scalar.activation(lg[:, U % 4, 0:n], lg[:, U % 4, 0:n], ACT.Exp, bias=st[:, 0, U % 4:U % 4 + 1],
                                     accum_out=st[:, 1, U % 4:U % 4 + 1]).then_inc(q["exp_done"], 1)

            def ssm(n):
                act.wait_ge(q["bcb_done"], n + 1)
                if n:
                    act.wait_ge(q["s_done"], n)
                nc.scalar.copy(bt[:], ps[:, B_Y, 0:P]).then_inc(q["bt_ready"], 1)
                act.wait_ge(acs_in, 16 * (n + 1))
                if n:
                    act.wait_ge(q["y_done"], n)
                nc.scalar.activation(ctd[:], acsb[:], ACT.Exp).then_inc(q["eacs_ready"], 1)
                act.wait_ge(q["dm_masked"], n + 1)
                nc.scalar.activation(dm[:], dm[:], ACT.Exp).then_inc(q["decay_ready"], 1)
            for j in range(PAIRS + 1):
                if j < PAIRS:
                    ssm(j)
                    proj(j, 0)
                U = (j - 1) * UNITS
                for u in range(UNITS):
                    if j >= 1:
                        exps(U + u)
                    if u == 1 and j < PAIRS:
                        proj(j, 1)
                if j < PAIRS:
                    proj(j, 2)
                if j >= 1:
                    act.wait_ge(q["pv_done"], j)
                    nc.scalar.copy(G.mixT[:, 8 + j - 1, :], ps[:, B_PV, :]).then_inc(q["pv_read"], 1)

        @block.tensor
        def _(pe):
            def proj(j, m, tiles=range(T)):
                n = 3 * j + m
                w = G.W.ring[:, (G.W.index[("qkv", j)] % RING) * SLOT:][:, m * KB * P:(m + 1) * KB * P]\
                    .rearrange("p (k n) -> p k n", n=P)
                if m == 0:
                    G.W.wait(pe, ("qkv", j))
                if n >= 2 and 0 in tiles:
                    pe.wait_ge(q["proj_read"], n - 1)
                out = ps[:, B_PROJ + n % 2, :]
                if m < 2:
                    for k in range(KB):
                        x = nc.tensor.matmul(out, w[:, k, :], G.hT[:, k, :], start=(k == 0), stop=(k == KB - 1))
                else:
                    for t in tiles:
                        for k in range(KB):
                            x = nc.tensor.matmul(out[:, t * P:(t + 1) * P], G.hT[:, k, t * P:(t + 1) * P], w[:, k, :],
                                                 start=(k == 0), stop=(k == KB - 1))
                if T - 1 in tiles:
                    x.then_inc(q["proj_done"], 1)
                    if m == 2:
                        pe.wait_ge(q["proj_done"], n + 1)
                        nc.tensor.nop().then_inc(G.W.used, 1)

            def logits(U):
                jj, u = U // UNITS, U % UNITS
                i, a = u // 2, u % 2
                if u == 0:
                    pe.wait_ge(q["proj_read"], 3 * jj + 3)
                if U >= 2:
                    pe.wait_ge(q["logits_read"], U - 1)
                n = (i + 1) * P
                out = ps[:, B_LOG + U % 2, 0:n]
                h = slice(HEAD * a, HEAD * a + HEAD)
                nc.tensor.matmul(out, qT[h, jj % 2, i * P:n], kT[h, jj % 2, 0:n], start=True, stop=False)
                nc.tensor.matmul(out[:, i * P:n], G.ident_bf[:], G.causal_bf[:], start=False, stop=True)\
                    .then_inc(q["logits_done"], 1)

            def turn(U):
                i = (U % UNITS) // 2
                pe.wait_ge(q["probs_ready"], U + 1)
                if U >= 1:
                    pe.wait_ge(q["pt_copied"], U)
                for b in range(i + 1):
                    x = nc.tensor.transpose(ps[:, B_TR, b * P:(b + 1) * P], lg[:, U % 4, b * P:(b + 1) * P], G.ident[:])
                x.then_inc(q["pt_done"], 1)

            def values(jj):
                pe.wait_ge(q["pt_copied"], UNITS * (jj + 1))
                if jj >= 1:
                    pe.wait_ge(q["pv_read"], jj)
                for b in range(T):
                    for a in range(2):
                        x = nc.tensor.matmul(ps[HEAD * a:HEAD * a + HEAD, B_PV, b * P:], vv[:, jj % 2, b, HEAD * a:HEAD * a + HEAD],
                                             pT[:, a, FROM[b]:FROM[b] + (T - b) * P], start=(b == 0), stop=(b == T - 1))
                x.then_inc(q["pv_done"], 1)

            def ssm_in(n):
                c, g = n // 2, n % 2
                at = slice(c * P, (c + 1) * P)
                if n >= 1:
                    pe.wait_ge(q["state_ready"], n)
                for b in range(4):
                    x = nc.tensor.transpose(ps[:, B_X, b * P:(b + 1) * P], G.xbcT[:, 4 * g + b, at], G.ident[:])
                x.then_inc(q["xt_done"], 1)
                if n >= 1:
                    pe.wait_ge(q["y_read"], n)
                nc.tensor.transpose(ps[:, B_Y, 0:P], G.xbcT[:, 8 + g, at], G.ident[:])
                nc.tensor.matmul(ps[:, B_Y, P:2 * P], G.xbcT[:, 8 + g, at], G.xbcT[:, 10 + g, at],
                                 start=True, stop=True).then_inc(q["bcb_done"], 1)

            def ssm_out(n):
                c, g = n // 2, n % 2
                pe.wait_ge(q["xc_ready"], n + 1)
                pe.wait_ge(q["bt_ready"], n + 1)
                pe.wait_ge(q["sc_ready"], n + 1)
                pe.wait_ge(q["ctd_ready"], n + 1)
                if c:
                    pe.wait_ge(q["state_ready"], n - 1)
                for b in range(4):
                    for a in range(2):
                        h = 2 * b + a
                        out = ps[HEAD * a:HEAD * a + HEAD, B_Y, b * P:(b + 1) * P]
                        x = nc.tensor.matmul(out, xc[:, h, :], dm[:, h, :], start=True, stop=(c == 0))
                        if c:
                            x = nc.tensor.matmul(out, state[:, g, h, :], ctd[:, h, :], start=False, stop=True)
                x.then_inc(q["y_done"], 1)
                pe.wait_ge(q["xcd_ready"], n + 1)
                nc.tensor.matmul(ps[:, B_X, :], bt[:], xcd[:].rearrange("p h w -> p (h w)"),
                                 start=True, stop=True).then_inc(q["s_done"], 1)

            for j in range(PAIRS + 1):
                new, old = j < PAIRS, j >= 1
                U = (j - 1) * UNITS
                if new:
                    ssm_in(j)
                    proj(j, 0)
                if old:
                    logits(U)
                    logits(U + 1)
                if new:
                    proj(j, 1)
                if old:
                    turn(U)
                    logits(U + 2)
                    turn(U + 1)
                    logits(U + 3)
                if new:
                    proj(j, 2, range(0, 2))
                if old:
                    turn(U + 2)
                    logits(U + 4)
                    turn(U + 3)
                    logits(U + 5)
                if new:
                    proj(j, 2, range(2, 4))
                if old:
                    turn(U + 4)
                    logits(U + 6)
                    turn(U + 5)
                    logits(U + 7)
                if new:
                    ssm_out(j)
                if old:
                    turn(U + 6)
                    turn(U + 7)
                    values(j - 1)

        @block.vector
        def _(dve):
            def maxima(U):
                jj, u = U // UNITS, U % UNITS
                i, a = u // 2, u % 2
                n = (i + 1) * P
                dve.wait_ge(q["logits_done"], U + 1)
                if u == 0:
                    dve.wait_ge(nb_in, 16 * (jj + 1))
                if U >= 4:
                    dve.wait_ge(q["pt_done"], U - 3)
                nc.vector.tensor_tensor_reduce(out=lg[:, U % 4, 0:n], in0=ps[:, B_LOG + U % 2, 0:n],
                                               in1=nb[:, a, 0:n], scale=1.0, scalar=-3.0e38, op0=ALU.add,
                                               op1=ALU.max, accum_out=st[:, 0, U % 4:U % 4 + 1]).then_inc(q["logits_read"], 1)
                dve.wait_ge(q["logits_read"], U + 1)
                nc.vector.tensor_scalar(st[:, 0, U % 4:U % 4 + 1], st[:, 0, U % 4:U % 4 + 1], -1.0, None,
                                        ALU.mult).then_inc(q["max_ready"], 1)

            def inverse(U):
                dve.wait_ge(q["exp_done"], U + 1)
                nc.vector.reciprocal(st[:, 2, U % 4:U % 4 + 1], st[:, 1, U % 4:U % 4 + 1]).then_inc(q["rinv_ready"], 1)

            def copy_turned(U):
                jj, u = U // UNITS, U % UNITS
                i, a = u // 2, u % 2
                dve.wait_ge(q["pt_done"], U + 1)
                if u < 2 and jj:
                    dve.wait_ge(q["pv_done"], jj)
                for b in range(i + 1):
                    to = FROM[b] + (i - b) * P
                    x = nc.vector.tensor_copy(pT[:, a, to:to + P], ps[:, B_TR, b * P:(b + 1) * P])
                x.then_inc(q["pt_copied"], 1)

            def ssm_in(n):
                c, g = n // 2, n % 2
                heads = slice(16 * c + 8 * g, 16 * c + 8 * g + 8)
                dve.wait_ge(q["xt_done"], n + 1)
                if n:
                    dve.wait_ge(q["y_done"], n)
                    dve.wait_ge(q["xcd_ready"], n)
                nc.vector.tensor_tensor(xc[:], ps[:, B_X, :].rearrange("p (h w) -> p h w", w=HEAD),
                                        bc_last(G.dt[:, c, 8 * g:8 * g + 8], HEAD), ALU.mult).then_inc(q["xc_ready"], 1)
                dve.wait_ge(acs_in, 16 * (n + 1))
                nc.vector.tensor_tensor(dm[:], acsb[:], bc_last(G.acs[:, heads], P),
                                        ALU.subtract).then_inc(q["dm_sub"], 1)
                dve.wait_ge(q["decay_ready"], n + 1)
                dve.wait_ge(q["bcb_done"], n + 1)
                nc.vector.tensor_tensor(dm[:], dm[:], bc_mid(ps[:, B_Y, P:2 * P], 8), ALU.mult)\
                    .then_inc(q["sc_ready"], 1)

            step = chain(dve, q["state_step"])

            def ssm_out(n):
                c, g = n // 2, n % 2
                at = slice(c * P, (c + 1) * P)
                dve.wait_ge(q["y_done"], n + 1)
                for b in range(4):
                    x = nc.vector.scalar_tensor_tensor(out=ytmp[:, b, :], in0=G.xbcT[:, 4 * g + b, at],
                                                       scalar=G.d_col[:, 4 * g + b:4 * g + b + 1],
                                                       in1=ps[:, B_Y, b * P:(b + 1) * P], op0=ALU.mult, op1=ALU.add)
                x.then_inc(q["y_read"], 1)
                dve.wait_ge(q["y_read"], n + 1)
                z = G.mixT[:, 4 * g:4 * g + 4, at]
                nc.vector.tensor_tensor(z, z, ytmp[:], ALU.mult).then_inc(q["ssm_out"], 1)
                dve.wait_ge(q["s_done"], n + 1)
                s_new = ps[:, B_X, :].rearrange("p (h w) -> p h w", w=HEAD)
                to = state[:, g]
                if c == 0:
                    nc.vector.tensor_copy(to, s_new).then_inc(q["state_ready"], 1)
                else:
                    step(nc.vector.tensor_tensor(to, to,
                                                 bc_last(G.decays[:, 16 * c + 8 * g:16 * c + 8 * g + 8], HEAD), ALU.mult))
                    nc.vector.tensor_tensor(to, to, s_new, ALU.add).then_inc(q["state_ready"], 1)

            for j in range(PAIRS + 1):
                new, old = j < PAIRS, j >= 1
                U = (j - 1) * UNITS
                if new:
                    ssm_in(j)
                if old:
                    for u in range(0, UNITS, 2):
                        maxima(U + u)
                        maxima(U + u + 1)
                        inverse(U + u)
                        inverse(U + u + 1)
                        if u < UNITS - 2:
                            copy_turned(U + u)
                            copy_turned(U + u + 1)
                if new:
                    ssm_out(j)
                if old:
                    copy_turned(U + UNITS - 2)
                    copy_turned(U + UNITS - 1)

class Norm:

    def __init__(self, nc, ctx, G, name, gain, shift):
        def sem(x):
            return G.sem(f"{name}_{x}")
        self.nc, self.G, self.gain, self.shift = nc, G, gain, shift
        self.u_ok, self.var_ok, self.root_ok = sem("u_ok"), sem("var_ok"), sem("root_ok")
        self.normed, self.step, self.gain_in = sem("normed"), sem("step"), sem("gain_in")
        self.gained, self.ready = sem("gained"), sem("ready")
        self.stats = ctx.enter_context(nc.sbuf_tensor(f"{name}_stats", [P, T, 2, 6], F32))
        self.mv = ctx.enter_context(nc.sbuf_tensor(f"{name}_mv", [P, T, 4], F32))
        self.gb = ctx.enter_context(nc.sbuf_tensor(f"{name}_gb", [P, 2, D], F32))
        self.chain = None

    def load(self, eng):
        eng.dma_start(self.gb[:, 0, :], self.gain.to_broadcast([P, D])).then_inc(self.gain_in, 16)
        eng.dma_start(self.gb[:, 1, :], self.shift.to_broadcast([P, D])).then_inc(self.gain_in, 16)

    def moments(self, dve, t):
        nc, X = self.nc, self.G.X
        if self.chain is None:
            self.chain = chain(dve, self.step)
        dve.wait_ge(self.u_ok, t + 1)
        nc.vector.bn_stats(self.stats[:, t, 0, :], X[:, t, 0:HALF])
        self.chain(nc.vector.bn_stats(self.stats[:, t, 1, :], X[:, t, HALF:]))
        self.chain(nc.vector.bn_aggr(self.mv[:, t, 0:2], self.stats[:, t].rearrange("p a b -> p (a b)")))
        nc.vector.tensor_scalar(self.mv[:, t, 2:3], self.mv[:, t, 1:2], EPS, None, ALU.add).then_inc(self.var_ok, 1)

    def root(self, act, t):
        act.wait_ge(self.var_ok, t + 1)
        self.nc.scalar.activation(self.mv[:, t, 2:3], self.mv[:, t, 2:3], ACT.Sqrt).then_inc(self.root_ok, 1)

    def norm(self, dve, t):
        nc, X = self.nc, self.G.X
        dve.wait_ge(self.root_ok, t + 1)
        self.chain(nc.vector.reciprocal(self.mv[:, t, 3:4], self.mv[:, t, 2:3]))
        nc.vector.tensor_scalar(X[:, t, :], X[:, t, :], self.mv[:, t, 0:1], self.mv[:, t, 3:4], ALU.subtract,
                                ALU.mult).then_inc(self.normed, 1)

    def gain_shift(self, pool, t):
        nc, X = self.nc, self.G.X
        if t == 0:
            pool.wait_ge(self.gain_in, 32)
        pool.wait_ge(self.normed, t + 1)
        nc.gpsimd.tensor_tensor(X[:, t, :], X[:, t, :], self.gb[:, 0, :], ALU.mult).then_inc(self.gained, 1)
        pool.wait_ge(self.gained, t + 1)
        nc.gpsimd.tensor_tensor(X[:, t, :], X[:, t, :], self.gb[:, 1, :], ALU.add).then_inc(self.ready, 1)


def stage_out(nc, A, G):
    with ExitStack() as ctx:
        def sb(name, shape, dt=F32):
            return ctx.enter_context(nc.sbuf_tensor(name, shape, dt))

        sem = G.sem
        ps = G.ps
        MB = 2 * KB
        sq = sb("squares", [P, 2, S])
        rr = sb("rms", [P, 2, S])
        sq_ok, ss_done, ss_read, rt_ok, r_ok, scaled = (sem(x) for x in (
            "sq_ok", "ss_done", "ss_read", "rms_root", "rms_ok", "scaled"))
        y_done, y_read, x_in, turned, h_ok = (sem(x) for x in ("out_done", "out_read", "x_again", "turned1", "h2_ok"))
        ln = Norm(nc, ctx, G, "ln1", A["ln1_g"][0:1, :], A["ln1_b"][0:1, :])
        block = ctx.enter_context(nc.Block())

        @block.sync
        def _(sp):
            G.W.upto(sp, G.W.index[("up", 0, 0)])
            for t in range(T):
                sp.dma_start(G.X[:, t, :], A["x"][0, t * P:(t + 1) * P, :]).then_inc(x_in, 16)
            ln.load(sp)
            G.W.upto(sp, G.W.index[("up", 0, 0)] + RING)

        @block.gpsimd
        def _(pool):
            for t in range(T):
                ln.gain_shift(pool, t)

        @block.scalar
        def _(act):
            for b in range(MB):
                if b >= 2:
                    act.wait_ge(ss_done, b - 1)
                nc.scalar.activation(sq[:, b % 2, :], G.mixT[:, b, :], ACT.Square).then_inc(sq_ok, 1)
            for m in range(2):
                act.wait_ge(ss_read, m + 1)
                nc.scalar.activation(rr[:, m, :], rr[:, m, :], ACT.Sqrt).then_inc(rt_ok, 1)
            for t in range(T):
                ln.root(act, t)
            for k in range(0, KB, 2):
                act.wait_ge(turned, KB)
                nc.scalar.activation(G.hT[:, k, :], ps[:, k, :], ACT.Identity, bias=G.mod2[:, k:k + 1],
                                     scale=G.mod2[:, KB + k:KB + k + 1]).then_inc(h_ok, 1)

        @block.tensor
        def _(pe):
            for b in range(MB):
                pe.wait_ge(sq_ok, b + 1)
                nc.tensor.matmul(ps[:, 6 + b // KB, :], G.ones[:], sq[:, b % 2, :], start=(b % KB == 0),
                                 stop=(b % KB == KB - 1)).then_inc(ss_done, 1)
            for t in range(T):
                for h in range(2):
                    if t == 3:
                        pe.wait_ge(ss_read, 2)
                    for k in range(MB):
                        if t == 0 and h == 0:
                            pe.wait_ge(scaled, k + 1)
                            G.W.wait(pe, ("out", k // 4))
                        w = G.W.view(("out", k // 4))
                        m = nc.tensor.matmul(ps[:, 2 * t + h, :], G.mixT[:, k, t * P:(t + 1) * P],
                                             w[:, k % 4, h * HALF:(h + 1) * HALF], start=(k == 0), stop=(k == MB - 1))
                m.then_inc(y_done, 1)
            pe.wait_ge(y_done, T)
            nc.tensor.nop().then_inc(G.W.used, 4)
            pe.wait_ge(y_read, T)
            for t in range(T):
                pe.wait_ge(ln.ready, t + 1)
                for k in range(KB):
                    m = nc.tensor.transpose(ps[:, k, t * P:(t + 1) * P], G.X[:, t, k * P:(k + 1) * P], G.ident[:])
                    if t == T - 1:
                        m.then_inc(turned, 1)

        @block.vector
        def _(dve):
            for m in range(2):
                dve.wait_ge(ss_done, KB * (m + 1))
                nc.vector.tensor_scalar(rr[:, m, :], ps[:, 6 + m, :], 1.0 / D, EPS, ALU.mult, ALU.add).then_inc(ss_read, 1)
            for m in range(2):
                dve.wait_ge(rt_ok, m + 1)
                nc.vector.reciprocal(rr[:, m, :], rr[:, m, :]).then_inc(r_ok, 1)
                dve.wait_ge(r_ok, m + 1)
                for b in range(KB):
                    nc.vector.scalar_tensor_tensor(out=G.mixT[:, KB * m + b, :], in0=G.mixT[:, KB * m + b, :],
                                                   scalar=G.pcol[:, R_SSMW + KB * m + b:R_SSMW + KB * m + b + 1],
                                                   in1=rr[:, m, :], op0=ALU.mult, op1=ALU.mult).then_inc(scaled, 1)
            dve.wait_ge(x_in, 16 * T)
            for t in range(T):
                dve.wait_ge(y_done, t + 1)
                y = G.Y[:, t % 2, :]
                nc.vector.tensor_tensor(y.rearrange("p (h n) -> p h n", h=2), ps[:, 2 * t:2 * t + 2, :],
                                        G.gate[:, 0, :].rearrange("p (h n) -> p h n", h=2), ALU.mult).then_inc(y_read, 1)
                dve.wait_ge(y_read, t + 1)
                nc.vector.scalar_tensor_tensor(out=G.X[:, t, :], in0=G.X[:, t, :], scalar=ALPHA, in1=y,
                                               op0=ALU.mult, op1=ALU.add).then_inc(ln.u_ok, 1)
                ln.moments(dve, t)
                ln.norm(dve, t)
            for k in range(1, KB, 2):
                dve.wait_ge(turned, KB)
                nc.vector.tensor_scalar(G.hT[:, k, :], ps[:, k, :], G.mod2[:, KB + k:KB + k + 1],
                                        G.mod2[:, k:k + 1], ALU.mult, ALU.add).then_inc(h_ok, 1)


def stage_ffn(nc, A, G):
    with ExitStack() as ctx:
        def sb(name, shape, dt=F32):
            return ctx.enter_context(nc.sbuf_tensor(name, shape, dt))

        sem = G.sem
        ps = G.ps
        aT = sb("hidden_T", [P, 2, KB, S])
        yacc = sb("ffn_out", [P, T, D])
        up_done, relu_ok, hid_ok, dn_done, dn_read, gated = (sem(x) for x in (
            "up_done", "relu_ok", "hid_ok", "down_done", "down_read", "gated2"))
        turned, h_ok = sem("turned2"), sem("x2T_ok")
        zeros, zeros_ok = sb("zeros", [P, D]), sem("zeros_ok")
        ln = Norm(nc, ctx, G, "ln2", A["ln2_g"][0:1, :], A["ln2_b"][0:1, :])
        block = ctx.enter_context(nc.Block())
        order = [(0, 0), (1, 0), (0, 1), (2, 0), (1, 1), (3, 0), (2, 1), (3, 1)]

        @block.sync
        def _(sp):
            ln.load(sp)
            G.W.upto(sp, G.W.index[("q2",)] + RING)
            sp.wait_ge(G.y_zeroed, 16 * (MAX_SLOTS - EXPERTS))

        @block.gpsimd
        def _(pool):
            nc.gpsimd.memset(zeros[:], 0.0).then_inc(zeros_ok, 1)
            for n in range(FG * KB):
                pool.wait_ge(relu_ok, n + 1)
                a = aT[:, (n // KB) % 2, n % KB, :]
                nc.gpsimd.tensor_tensor(a, a, a, ALU.mult).then_inc(hid_ok, 1)
            for t in range(T):
                ln.gain_shift(pool, t)

        @block.scalar
        def _(act):
            act.wait_ge(zeros_ok, 1)
            for i in range(EXPERTS, MAX_SLOTS):
                act.dma_start(G.y_dram[i * CAP:(i + 1) * CAP, :], zeros[:]).then_inc(G.y_zeroed, 16)
            for n in range(FG * KB):
                g = n // KB
                act.wait_ge(up_done, n + 1)
                if g >= 2:
                    act.wait_ge(dn_done, KB * (g - 1))
                nc.scalar.activation(aT[:, g % 2, n % KB, :], ps[:, n % 4, :], ACT.Relu).then_inc(relu_ok, 1)
            for t in range(T):
                ln.root(act, t)
            act.wait_ge(turned, KB)
            for k in range(0, KB, 2):
                nc.scalar.copy(G.hT[:, k, :], ps[:, k, :]).then_inc(h_ok, 1)

        @block.tensor
        def _(pe):
            def up(g):
                for b in range(KB):
                    n = g * KB + b
                    if b % 4 == 0:
                        G.W.wait(pe, ("up", g, b // 4))
                    w = G.W.view(("up", g, b // 4))
                    if n >= 4:
                        pe.wait_ge(relu_ok, n - 3)
                    for k in range(KB):
                        m = nc.tensor.matmul(ps[:, n % 4, :], w[:, k, (b % 4) * P:(b % 4 + 1) * P], G.hT[:, k, :],
                                             start=(k == 0), stop=(k == KB - 1))
                    m.then_inc(up_done, 1)
                    if b % 4 == 3:
                        pe.wait_ge(up_done, n + 1)
                        nc.tensor.nop().then_inc(G.W.used, 1)

            def down(g):
                pe.wait_ge(hid_ok, KB * (g + 1))
                for h in range(2):
                    G.W.wait(pe, ("down", g, h))
                for i in range(KB):
                    n = g * KB + i
                    t, h = i // 2, i % 2
                    if n >= 4:
                        pe.wait_ge(dn_read, n - 3)
                    for k in range(KB):
                        w = G.W.view(("down", g, k // 4))
                        m = nc.tensor.matmul(ps[:, 4 + n % 4, :], aT[:, g % 2, k, t * P:(t + 1) * P],
                                             w[:, k % 4, h * HALF:(h + 1) * HALF], start=(k == 0), stop=(k == KB - 1))
                    m.then_inc(dn_done, 1)
                pe.wait_ge(dn_done, KB * (g + 1))
                nc.tensor.nop().then_inc(G.W.used, 2)
            for g, kind in order:
                down(g) if kind else up(g)
            pe.wait_ge(dn_read, FG * KB)
            for t in range(T):
                pe.wait_ge(ln.ready, t + 1)
                for k in range(KB):
                    m = nc.tensor.transpose(ps[:, k, t * P:(t + 1) * P], G.X[:, t, k * P:(k + 1) * P], G.ident[:])
                    if t == T - 1:
                        m.then_inc(turned, 1)

        @block.vector
        def _(dve):
            def add(n):
                g, i = n // KB, n % KB
                t, h = i // 2, i % 2
                y = yacc[:, t, h * HALF:(h + 1) * HALF]
                dve.wait_ge(dn_done, n + 1)
                if g == 0:
                    nc.vector.tensor_copy(y, ps[:, 4 + n % 4, :]).then_inc(dn_read, 1)
                else:
                    nc.vector.tensor_tensor(y, y, ps[:, 4 + n % 4, :], ALU.add).then_inc(dn_read, 1)
            for n in range((FG - 1) * KB):
                add(n)
            for t in range(T):
                add((FG - 1) * KB + 2 * t)
                add((FG - 1) * KB + 2 * t + 1)
                dve.wait_ge(dn_read, (FG - 1) * KB + 2 * t + 2)
                nc.vector.tensor_tensor(yacc[:, t, :], yacc[:, t, :], G.gate[:, 1, :], ALU.mult).then_inc(gated, 1)
                dve.wait_ge(gated, t + 1)
                nc.vector.scalar_tensor_tensor(out=G.X[:, t, :], in0=G.X[:, t, :], scalar=ALPHA, in1=yacc[:, t, :],
                                               op0=ALU.mult, op1=ALU.add).then_inc(ln.u_ok, 1)
                ln.moments(dve, t)
                ln.norm(dve, t)
            for k in range(1, KB, 2):
                dve.wait_ge(turned, KB)
                nc.vector.tensor_copy(G.hT[:, k, :], ps[:, k, :]).then_inc(h_ok, 1)

def stage_second(nc, A, G):
    NB = 2 * T
    with ExitStack() as ctx:
        def sb(name, shape, dt=F32):
            return ctx.enter_context(nc.sbuf_tensor(name, shape, dt))

        sem = G.sem
        ps = G.ps
        qT = sb("q2T", [P, 4, S])
        kT = sb("k2T", [P, S])
        vt = sb("v2", [P, T, P])
        u = sb("u2", [P, T, HALF])
        g = sb("g2", [P, T, HALF])
        gx = sb("g2_sq", [P, T, HALF])
        mixT = sb("mix2T", [P, KB, S])
        pr = sb("probs2", [P, 4, 2 * P])
        pT = sb("probs2_T", [P, 4, 2, P])
        st = sb("softmax2", [P, 6, 4])
        sinks = sb("sink_row", [P, Q_HEADS])
        wsp = sb("w_spatial", [P, 8, P])
        wspT = sb("w_spatial_T", [P, 8, P])
        bsp_rows = sb("b_spatial_rows", [8, P])
        bsp = sb("b_spatial_cols", [P, 8])
        tb = sb("token_bias", [P, 1152])
        lnr = sb("gate_norm_rows", [P, 2, HALF])
        gs = sb("gate_stats", [P, 4, 32])
        b_out = sb("b_out_row", [P, D])
        names = ("params fm_done q_ok k_ok v_ok tm_done tm_read gelu_ok lg_done max_ok neg_ok exp_ok esink_ok sum_ok rinv_ok "
                 "p_ok pt_done pt_read pv_done pv_read wt_done wt_ok gstep gsq_ok groot_ok gn_mid gn_mid2 gn_ok sg_done sg_ok "
                 "sgT_done sgT_ok y_done y_read turned h_ok sm_step out_b").split()
        q = {x: sem("s2_" + x) for x in names}
        ln = Norm(nc, ctx, G, "ln1b", A["ln1_g_2"][0:1, :], A["ln1_b_2"][0:1, :])
        block = ctx.enter_context(nc.Block())

        @block.sync
        def _(sp):
            w = [(sinks[:], A["sinks_2"][0:1, :].to_broadcast([P, Q_HEADS])),
                 (tb[:], A["b_in_2"][0:1, 640:1792].to_broadcast([P, 1152])),
                 (wsp[:], A["w_spatial_2"][0].rearrange("g t s -> t g s")),
                 (bsp_rows[:], A["b_spatial_2"][0]),
                 (lnr[:, 0, :], A["ln_v_g_2"][0:1, :].to_broadcast([P, HALF])),
                 (lnr[:, 1, :], A["ln_v_b_2"][0:1, :].to_broadcast([P, HALF])),
                 (b_out[:], A["b_out_2"][0:1, :].to_broadcast([P, D]))]
            for dst, src in w:
                sp.dma_start(dst, src).then_inc(q["params"], 16)
            ln.load(sp)
            G.W.upto(sp, len(G.W.plan))
            for t in range(T):
                sp.wait_ge(ln.ready, t + 1)
                sp.dma_start(G.h_dram[t * P:(t + 1) * P, :], G.X[:, t, :]).then_inc(G.h_out, 16)

        @block.gpsimd
        def _(pool):
            pool.wait_ge(q["params"], 16 * 7)
            for n in range(NB):
                blk = n // 2
                lo = 0 if blk else P
                pool.wait_ge(q["rinv_ok"], n + 1)
                nc.gpsimd.tensor_tensor(pr[:, :, lo:], pr[:, :, lo:], bc_last(st[:, 5, :], 2 * P - lo), ALU.mult)\
                    .then_inc(q["p_ok"], 1)
            pool.wait_ge(q["gn_mid"], 1)
            for i, op in ((0, ALU.mult), (1, ALU.add)):
                nc.gpsimd.tensor_tensor(g[:], g[:], bc_mid(lnr[:, i, :], T), op).then_inc(q["gn_ok"], 1)
                pool.wait_ge(q["gn_ok"], i + 1)
            for t in range(T):
                ln.gain_shift(pool, t)

        @block.scalar
        def _(act):
            def gelu(n):
                act.wait_ge(q["tm_read"], n + 1)
                x = (u if n < T else g)[:, n % T, :]
                nc.scalar.activation(x, x, ACT.Gelu_apprx_tanh).then_inc(q["gelu_ok"], 1)

            for n in range(NB):
                lo = 0 if n // 2 else P
                act.wait_ge(q["neg_ok"], n + 1)
                if n:
                    act.wait_ge(q["pt_done"], n)
                for h in range(4):
                    x = nc.scalar.activation(pr[:, h, lo:], ps[:, 2 + h // 2, (h % 2) * 256 + lo:(h % 2) * 256 + 256],
                                             ACT.Exp, bias=st[:, 1, h:h + 1], accum_out=st[:, 2, h:h + 1])
                x.then_inc(q["exp_ok"], 1)
                nc.scalar.activation(st[:, 3, :], st[:, 3, :], ACT.Exp).then_inc(q["esink_ok"], 1)
                act.wait_ge(q["pv_done"], n + 1)
                nc.scalar.copy(mixT[:, 2 * (n % 2):2 * (n % 2) + 2, (n // 2) * P:(n // 2 + 1) * P],
                               ps[:, 6, 0:2 * P].rearrange("p (b n) -> p b n", n=P)).then_inc(q["pv_read"], 1)
            for n in range(2 * T):
                gelu(n)
            act.wait_ge(q["gstep"], 2)
            nc.scalar.activation(gx[:], g[:], ACT.Square).then_inc(q["gsq_ok"], 1)
            act.wait_ge(q["gstep"], 4)
            nc.scalar.activation(gs[:, 2, :], gs[:, 2, :], ACT.Sqrt).then_inc(q["groot_ok"], 1)
            for b in range(2):
                act.wait_ge(q["sgT_done"], 2 * b + 2)
                nc.scalar.copy(mixT[:, 4 + 2 * b + 1, :], ps[:, 4 + 2 * b + 1, :]).then_inc(q["sgT_ok"], 1)
            for t in range(T):
                ln.root(act, t)
            for k in range(0, KB, 2):
                act.wait_ge(q["turned"], KB)
                nc.scalar.copy(G.hT[:, k, :], ps[:, k, :]).then_inc(q["h_ok"], 1)

        @block.tensor
        def _(pe):
            G.W.wait(pe, ("q2",))
            w = G.W.view(("q2",))
            for j in range(4):
                for k in range(KB):
                    for a in range(2):
                        m = nc.tensor.matmul(ps[HEAD * a:HEAD * a + HEAD, j, :], w[:, k, 256 * a + HEAD * j:256 * a + HEAD * (j + 1)],
                                             G.hT[:, k, :], start=(k == 0), stop=(k == KB - 1))
                m.then_inc(q["fm_done"], 1)
            pe.wait_ge(q["fm_done"], 4)
            nc.tensor.nop().then_inc(G.W.used, 1)
            G.W.wait(pe, ("kv2",))
            w = G.W.view(("kv2",))
            for k in range(KB):
                m = nc.tensor.matmul(ps[:, 4, :], w[:, k, 0:P], G.hT[:, k, :], start=(k == 0), stop=(k == KB - 1))
            m.then_inc(q["fm_done"], 1)
            for t in range(T):
                for k in range(KB):
                    m = nc.tensor.matmul(ps[:, 5, t * P:(t + 1) * P], G.hT[:, k, t * P:(t + 1) * P], w[:, k, P:2 * P],
                                         start=(k == 0), stop=(k == KB - 1))
            m.then_inc(q["fm_done"], 1)
            pe.wait_ge(q["fm_done"], 6)
            nc.tensor.nop().then_inc(G.W.used, 1)

            def token_major(n):
                key = ("u2",) if n < T else ("g2",)
                G.W.wait(pe, key)
                w = G.W.view(key)
                t = n % T
                if n >= 2:
                    pe.wait_ge(q["tm_read"], n - 1)
                for k in range(KB):
                    m = nc.tensor.matmul(ps[:, n % 2, :], G.hT[:, k, t * P:(t + 1) * P], w[:, k, :],
                                         start=(k == 0), stop=(k == KB - 1))
                m.then_inc(q["tm_done"], 1)
                if t == T - 1:
                    pe.wait_ge(q["tm_done"], n + 1)
                    nc.tensor.nop().then_inc(G.W.used, 1)

            def logits(n):
                blk, kv = n // 2, n % 2
                if n:
                    pe.wait_ge(q["exp_ok"], n)
                r = slice(HEAD * kv, HEAD * kv + HEAD)
                for h in range(4):
                    out = ps[:, 2 + h // 2, (h % 2) * 256:(h % 2) * 256 + 256]
                    query = qT[r, h, blk * P:(blk + 1) * P]
                    if blk:
                        nc.tensor.matmul(out, query, kT[r, (blk - 1) * P:(blk + 1) * P], start=True, stop=False)
                        nc.tensor.matmul(out[:, 0:P], G.ident_bf[:], G.before_bf[:], start=False, stop=False)
                    else:
                        nc.tensor.matmul(out[:, P:], query, kT[r, 0:P], start=True, stop=False)
                    m = nc.tensor.matmul(out[:, P:], G.ident_bf[:], G.causal_bf[:], start=False, stop=True)
                m.then_inc(q["lg_done"], 1)

            def turn(n):
                pe.wait_ge(q["p_ok"], n + 1)
                if n:
                    pe.wait_ge(q["pt_read"], n)
                for h in range(4):
                    for b in range(0 if n // 2 else 1, 2):
                        m = nc.tensor.transpose(ps[:, 4 + h // 2, ((h % 2) * 2 + b) * P:((h % 2) * 2 + b + 1) * P],
                                                pr[:, h, b * P:(b + 1) * P], G.ident[:])
                m.then_inc(q["pt_done"], 1)

            def values(n):
                blk, kv = n // 2, n % 2
                pe.wait_ge(q["pt_read"], n + 1)
                if n:
                    pe.wait_ge(q["pv_read"], n)
                for h in range(4):
                    out = ps[HEAD * (h % 2):HEAD * (h % 2) + HEAD, 6, (h // 2) * P:(h // 2 + 1) * P]
                    first = 0 if blk else 1
                    for b in range(first, 2):
                        m = nc.tensor.matmul(out, vt[:, blk - 1 + b, HEAD * kv:HEAD * kv + HEAD], pT[:, h, b, :],
                                             start=(b == first), stop=(b == 1))
                m.then_inc(q["pv_done"], 1)

            pe.wait_ge(q["q_ok"], 4)
            pe.wait_ge(q["k_ok"], 1)
            pe.wait_ge(q["v_ok"], 1)
            for n in range(NB):
                logits(n)
                token_major(n)
                turn(n)
                values(n)
            pe.wait_ge(q["params"], 16 * 7)
            for h in range(8):
                nc.tensor.transpose(ps[:, 4 + h // 4, (h % 4) * P:(h % 4 + 1) * P], wsp[:, h, :], G.ident[:])
            nc.tensor.transpose(ps[:, 7, 0:8], bsp_rows[:], G.ident[0:8, 0:8]).then_inc(q["wt_done"], 1)
            pe.wait_ge(q["gn_ok"], 2)
            pe.wait_ge(q["wt_ok"], 3)
            for h in range(8):
                m = nc.tensor.matmul(ps[:, h // 2, (h % 2) * 256:(h % 2) * 256 + 256].rearrange("p (c n) -> p c n", n=HEAD),
                                     wspT[:, h, :], g[:, :, h * HEAD:(h + 1) * HEAD], start=True, stop=True)
                m.then_inc(q["sg_done"], 1)
            pe.wait_ge(q["sg_ok"], 8)
            for b in range(4):
                for t in range(T):
                    m = nc.tensor.transpose(ps[:, 4 + b, t * P:(t + 1) * P], u[:, t, b * P:(b + 1) * P], G.ident[:])
                m.then_inc(q["sgT_done"], 1)
            pe.wait_ge(q["sgT_ok"], 4)
            for h in range(2):
                G.W.wait(pe, ("out2", h))
            for t in range(T):
                for h in range(2):
                    for k in range(KB):
                        w = G.W.view(("out2", k // 4))
                        m = nc.tensor.matmul(ps[:, 2 * t + h, :], mixT[:, k, t * P:(t + 1) * P],
                                             w[:, k % 4, h * HALF:(h + 1) * HALF], start=(k == 0), stop=(k == KB - 1))
                m.then_inc(q["y_done"], 1)
            pe.wait_ge(q["y_read"], T)
            for t in range(T):
                pe.wait_ge(ln.ready, t + 1)
                for k in range(KB):
                    m = nc.tensor.transpose(ps[:, k, t * P:(t + 1) * P], G.X[:, t, k * P:(k + 1) * P], G.ident[:])
                    if t == T - 1:
                        m.then_inc(q["turned"], 1)

        @block.vector
        def _(dve):
            for j in range(4):
                dve.wait_ge(q["fm_done"], j + 1)
                nc.vector.tensor_scalar(qT[:, j, :], ps[:, j, :], G.pcol[:, R_B2 + j:R_B2 + j + 1], HEAD ** -0.5,
                                        ALU.add, ALU.mult).then_inc(q["q_ok"], 1)
            dve.wait_ge(q["fm_done"], 5)
            nc.vector.tensor_scalar(kT[:], ps[:, 4, :], G.pcol[:, R_B2 + 4:R_B2 + 5], None, ALU.add).then_inc(q["k_ok"], 1)
            dve.wait_ge(q["fm_done"], 6)
            dve.wait_ge(q["params"], 16 * 7)
            nc.vector.tensor_tensor(vt[:], ps[:, 5, :].rearrange("p (t n) -> p t n", n=P), bc_mid(tb[:, 0:P], T),
                                    ALU.add).then_inc(q["v_ok"], 1)

            def softmax(n):
                blk, kv = n // 2, n % 2
                lo = 0 if blk else P
                sink = sinks[:, 4 * kv:4 * kv + 4]
                step = lambda ins: sm(ins)
                dve.wait_ge(q["lg_done"], n + 1)
                for h in range(2):
                    x = nc.vector.tensor_reduce(st[:, 0, 2 * h:2 * h + 2],
                                                ps[:, 2 + h, :].rearrange("p (h n) -> p h n", n=256)[:, :, lo:],
                                                AX_X, ALU.max)
                step(x)
                step(nc.vector.tensor_tensor(st[:, 0, :], st[:, 0, :], sink, ALU.max))
                step(nc.vector.tensor_tensor(st[:, 3, :], sink, st[:, 0, :], ALU.subtract))
                nc.vector.tensor_scalar(st[:, 1, :], st[:, 0, :], -1.0, None, ALU.mult).then_inc(q["neg_ok"], 1)

            def inverse(n):
                dve.wait_ge(q["esink_ok"], n + 1)
                dve.wait_ge(q["exp_ok"], n + 1)
                sm(nc.vector.tensor_tensor(st[:, 4, :], st[:, 2, :], st[:, 3, :], ALU.add))
                nc.vector.reciprocal(st[:, 5, :], st[:, 4, :]).then_inc(q["rinv_ok"], 1)

            sm = chain(dve, q["sm_step"])
            for n in range(NB):
                softmax(n)
                inverse(n)
                dve.wait_ge(q["tm_done"], n + 1)
                x = (u if n < T else g)[:, n % T, :]
                c0 = P if n < T else P + HALF
                nc.vector.tensor_tensor(x, ps[:, n % 2, :], tb[:, c0:c0 + HALF], ALU.add).then_inc(q["tm_read"], 1)
                dve.wait_ge(q["pt_done"], n + 1)
                first = 0 if n // 2 else 1
                if n:
                    dve.wait_ge(q["pv_done"], n)
                for h in range(2):
                    x = nc.vector.tensor_copy(pT[:, 2 * h:2 * h + 2, first:, :],
                                              ps[:, 4 + h, :].rearrange("p (h b n) -> p h b n", b=2, n=P)[:, :, first:, :])
                x.then_inc(q["pt_read"], 1)
            dve.wait_ge(q["wt_done"], 1)
            for h in range(2):
                nc.vector.tensor_tensor(wspT[:, 4 * h:4 * h + 4, :], ps[:, 4 + h, :].rearrange("p (g n) -> p g n", n=P),
                                        bc_mid(G.tri[:], 4), ALU.mult).then_inc(q["wt_ok"], 1)
            nc.vector.tensor_copy(bsp[:], ps[:, 7, 0:8]).then_inc(q["wt_ok"], 1)
            g3 = g[:].rearrange("p t (a n) -> p (t a) n", n=HEAD)
            gx3 = gx[:].rearrange("p t (a n) -> p (t a) n", n=HEAD)
            dve.wait_ge(q["gelu_ok"], 2 * T)
            step = chain(dve, q["gstep"])
            nc.vector.tensor_reduce(gs[:, 0, :], g3, AX_X, ALU.add).then_inc(q["gn_mid2"], 1)
            dve.wait_ge(q["gn_mid2"], 1)
            step(nc.vector.tensor_scalar(gs[:, 1, :], gs[:, 0, :], 1.0 / HEAD, None, ALU.mult))
            step(nc.vector.tensor_tensor(g3, g3, bc_last(gs[:, 1, :], HEAD), ALU.subtract))
            dve.wait_ge(q["gsq_ok"], 1)
            step(nc.vector.tensor_reduce(gs[:, 0, :], gx3, AX_X, ALU.add))
            step(nc.vector.tensor_scalar(gs[:, 2, :], gs[:, 0, :], 1.0 / HEAD, EPS, ALU.mult, ALU.add))
            dve.wait_ge(q["groot_ok"], 1)
            step(nc.vector.reciprocal(gs[:, 3, :], gs[:, 2, :]))
            nc.vector.tensor_tensor(g3, g3, bc_last(gs[:, 3, :], HEAD), ALU.mult).then_inc(q["gn_mid"], 1)
            for h in range(8):
                dve.wait_ge(q["sg_done"], 2 * (h // 2) + 2)
                uu = u[:, :, h * HEAD:(h + 1) * HEAD]
                nc.vector.scalar_tensor_tensor(out=uu, in0=ps[:, h // 2, (h % 2) * 256:(h % 2) * 256 + 256]
                                               .rearrange("p (c n) -> p c n", n=HEAD), scalar=bsp[:, h:h + 1], in1=uu,
                                               op0=ALU.add, op1=ALU.mult).then_inc(q["sg_ok"], 1)
            for b in range(2):
                dve.wait_ge(q["sgT_done"], 2 * b + 1)
                nc.vector.tensor_copy(mixT[:, 4 + 2 * b, :], ps[:, 4 + 2 * b, :]).then_inc(q["sgT_ok"], 1)
            for t in range(T):
                dve.wait_ge(q["y_done"], t + 1)
                y = G.Y[:, t % 2, :]
                nc.vector.tensor_tensor(y.rearrange("p (h n) -> p h n", h=2), ps[:, 2 * t:2 * t + 2, :],
                                        b_out[:].rearrange("p (h n) -> p h n", h=2), ALU.add).then_inc(q["y_read"], 1)
                dve.wait_ge(q["y_read"], t + 1)
                nc.vector.scalar_tensor_tensor(out=G.X[:, t, :], in0=G.X[:, t, :], scalar=ALPHA, in1=y,
                                               op0=ALU.mult, op1=ALU.add).then_inc(ln.u_ok, 1)
                ln.moments(dve, t)
                ln.norm(dve, t)
            for k in range(1, KB, 2):
                dve.wait_ge(q["turned"], KB)
                nc.vector.tensor_copy(G.hT[:, k, :], ps[:, k, :]).then_inc(q["h_ok"], 1)

def stage_route(nc, A, G):
    TK = T * TOP_K
    E = EXPERTS
    with ExitStack() as ctx:
        def sb(name, shape, dt=F32):
            return ctx.enter_context(nc.sbuf_tensor(name, shape, dt))

        sem = G.sem
        ps = G.ps
        w_r = sb("w_router", [P, KB, E])
        b_r = sb("b_router", [P, E])
        lg = sb("router_logits", [P, T, E])
        top = sb("top8", [P, T, 8])
        idx = sb("top8_index", [P, T, 8], U32)
        idxf = sb("choice_expert", [P, T, TOP_K])
        neg = sb("neg_top", [P, T])
        ex = sb("gate_exp", [P, T, TOP_K])
        gsum = sb("gate_sum", [P, 2, T])
        iota_i = sb("iota_int", [P, P], I32)
        iota = sb("iota", [P, P])
        tok_i = sb("token_int", [P, T], I32)
        tok = sb("token", [P, T])
        oh = sb("choice_onehot", [P, TK, E])
        pick = sb("picked", [P, TK, E])
        mem = sb("members", [P, T, E])
        pos = sb("position", [P, T, E])
        tmp = sb("route_tmp", [P, T, E])
        cnt = sb("counts", [P, E])
        nb = sb("slots_of", [P, 2, E])
        base = sb("slot_base", [P, E])
        over = sb("over", [P, T, E])
        sl = sb("choice_slot", [P, TK])
        col = sb("choice_col", [P, TK])
        rowf = sb("choice_rowf", [P, TK])
        colhot = sb("col_onehot", [P, 2, P])
        slothot = sb("slot_token", [P, 2, LIST])
        cmp_ = sb("slot_compare", [P, LIST, E])
        sef = sb("slot_expertf", [P, LIST])
        names = "in lg_done iota_ok step exp_ok mem_ok cnt_done hot_ok hot_used list_done neg_ok".split()
        q = {x: sem("rt_" + x) for x in names}
        block = ctx.enter_context(nc.Block())

        @block.sync
        def _(sp):
            sp.dma_start(w_r[:], A["w_router_2"][0].rearrange("(k p) n -> p k n", p=P)).then_inc(q["in"], 16)
            sp.dma_start(b_r[:], A["b_router_2"][0:1, :].to_broadcast([P, E])).then_inc(q["in"], 16)
            G.experts.prefetch(sp)

        @block.gpsimd
        def _(pool):
            nc.gpsimd.iota(iota_i[:], pattern=[[1, P]], base=0, channel_multiplier=0).then_inc(q["iota_ok"], 1)
            nc.gpsimd.iota(tok_i[:], pattern=[[P, T]], base=0, channel_multiplier=1).then_inc(q["iota_ok"], 1)

        @block.scalar
        def _(act):
            for t in range(T):
                act.wait_ge(q["neg_ok"], t + 1)
                nc.scalar.activation(ex[:, t, :], top[:, t, 0:TOP_K], ACT.Exp, bias=neg[:, t:t + 1],
                                     accum_out=gsum[:, 0, t:t + 1]).then_inc(q["exp_ok"], 1)

        @block.tensor
        def _(pe):
            pe.wait_ge(q["in"], 32)
            for t in range(T):
                for k in range(KB):
                    m = nc.tensor.matmul(ps[:, 0, t * E:(t + 1) * E], G.hT[:, k, t * P:(t + 1) * P], w_r[:, k, :],
                                         start=(k == 0), stop=(k == KB - 1))
            m.then_inc(q["lg_done"], 1)
            pe.wait_ge(q["mem_ok"], 1)
            for t in range(T):
                for b in range(t):
                    nc.tensor.matmul(ps[:, 1, t * E:(t + 1) * E], G.ones[:], mem[:, b, :], start=(b == 0), stop=False)
                nc.tensor.matmul(ps[:, 1, t * E:(t + 1) * E], G.strict[:], mem[:, t, :], start=(t == 0), stop=True)
            for t in range(T):
                m = nc.tensor.matmul(ps[:, 2, 0:E], G.ones[:], mem[:, t, :], start=(t == 0), stop=(t == T - 1))
            m.then_inc(q["cnt_done"], 1)
            for c in range(TK):
                pe.wait_ge(q["hot_ok"], c + 1)
                nc.tensor.matmul(ps[:, 3, 0:LIST], colhot[:, c % 2, :], slothot[:, c % 2, :], start=(c == 0),
                                 stop=(c == TK - 1)).then_inc(q["hot_used"], 1)

        @block.vector
        def _(dve):
            step = chain(dve, q["step"])
            dve.wait_ge(q["iota_ok"], 2)
            nc.vector.tensor_copy(iota[:], iota_i[:])
            nc.vector.tensor_copy(tok[:], tok_i[:])
            dve.wait_ge(q["lg_done"], 1)
            dve.wait_ge(q["in"], 32)
            step(nc.vector.tensor_tensor(lg[:], ps[:, 0, 0:T * E].rearrange("p (t e) -> p t e", e=E),
                                         bc_mid(b_r[:], T), ALU.add))
            for t in range(T):
                step(nc.vector.max(top[:, t, :], lg[:, t, :]))
                nc.vector.max_index(idx[:, t, :], top[:, t, :], lg[:, t, :])
                nc.vector.tensor_scalar(neg[:, t:t + 1], top[:, t, 0:1], -1.0, None, ALU.mult).then_inc(q["neg_ok"], 1)
            dve.wait_ge(q["neg_ok"], T)
            step(nc.vector.tensor_copy(idxf[:], idx[:, :, 0:TOP_K]))
            step(nc.vector.tensor_tensor(oh[:], bc_mid(iota[:, 0:E], TK), bc_last(idxf[:].rearrange("p t k -> p (t k)"), E),
                                         ALU.is_equal))
            nc.vector.tensor_reduce(mem[:], oh[:].rearrange("p (t k) e -> p t e k", k=TOP_K), AX_X, ALU.add)\
                .then_inc(q["mem_ok"], 1)
            dve.wait_ge(q["exp_ok"], T)
            step(nc.vector.reciprocal(gsum[:, 1, :], gsum[:, 0, :]))
            nc.vector.tensor_tensor(G.gates[:], ex[:], bc_last(gsum[:, 1, :], TOP_K), ALU.mult)
            dve.wait_ge(q["cnt_done"], 1)
            step(nc.vector.tensor_copy(cnt[:], ps[:, 2, 0:E]))
            nc.vector.tensor_copy(pos[:], ps[:, 1, 0:T * E].rearrange("p (t e) -> p t e", e=E))
            step(nc.vector.tensor_scalar(nb[:, 0, :], cnt[:], float(CAP), 1.0, ALU.is_gt, ALU.add))
            for b in range(2, T):
                step(nc.vector.scalar_tensor_tensor(out=nb[:, 0, :], in0=cnt[:], scalar=float(b * CAP), in1=nb[:, 0, :],
                                                    op0=ALU.is_gt, op1=ALU.add))
            step(nc.vector.tensor_copy(base[:], nb[:, 0, :]))
            a, s = 0, 1
            while s < E:
                nc.vector.tensor_copy(nb[:, 1 - a, 0:s], nb[:, a, 0:s])
                step(nc.vector.tensor_tensor(nb[:, 1 - a, s:], nb[:, a, s:], nb[:, a, 0:E - s], ALU.add))
                a, s = 1 - a, 2 * s
            upto = nb[:, a, :]
            step(nc.vector.tensor_tensor(base[:], upto, base[:], ALU.subtract))
            nc.vector.tensor_scalar(G.last_slot[:], upto[:, E - 1:E], -1.0, None, ALU.add)
            step(nc.vector.tensor_tensor(cmp_[:], bc_mid(upto, LIST), bc_last(iota[:, 0:LIST], E), ALU.is_le))
            step(nc.vector.tensor_reduce(sef[:], cmp_[:], AX_X, ALU.add))
            nc.vector.tensor_scalar(G.slot_expert[:], sef[:], float(E - 1), None, ALU.min)
            step(nc.vector.tensor_scalar(over[:], pos[:], float(CAP), None, ALU.is_ge))
            for b in range(2, T):
                step(nc.vector.scalar_tensor_tensor(out=over[:], in0=pos[:], scalar=float(b * CAP), in1=over[:],
                                                    op0=ALU.is_ge, op1=ALU.add))
            step(nc.vector.scalar_tensor_tensor(out=pos[:], in0=over[:], scalar=-float(CAP), in1=pos[:], op0=ALU.mult,
                                                op1=ALU.add))
            step(nc.vector.tensor_tensor(over[:], over[:], bc_mid(base[:], T), ALU.add))
            oh4 = oh[:].rearrange("p (t k) e -> p t k e", k=TOP_K)
            pick4 = pick[:].rearrange("p (t k) e -> p t k e", k=TOP_K)
            for src, dst in ((over, sl), (pos, col)):
                for t in range(T):
                    x = nc.vector.tensor_tensor(pick4[:, t], oh4[:, t], bc_mid(src[:, t, :], TOP_K), ALU.mult)
                step(x)
                step(nc.vector.tensor_reduce(dst[:], pick[:], AX_X, ALU.add))
            for c in range(TK):
                if c >= 2:
                    dve.wait_ge(q["hot_used"], c - 1)
                nc.vector.tensor_scalar(colhot[:, c % 2, :], iota[:], col[:, c:c + 1], None, ALU.is_equal)
                nc.vector.tensor_scalar(slothot[:, c % 2, :], iota[:, 0:LIST], sl[:, c:c + 1],
                                        tok[:, c // TOP_K:c // TOP_K + 1], ALU.is_equal, ALU.mult).then_inc(q["hot_ok"], 1)
            step(nc.vector.scalar_tensor_tensor(out=rowf[:], in0=sl[:], scalar=float(CAP), in1=col[:], op0=ALU.mult,
                                                op1=ALU.add))
            nc.vector.tensor_copy(G.choice_row[:], rowf[:])
            dve.wait_ge(q["hot_used"], TK)
            step(nc.vector.tensor_copy(G.slot_tokens[:], ps[:, 3, 0:LIST]))


class Experts:
    PLACES = 6

    def __init__(self, nc, ctx, A):
        self.A = A
        self.ring = ctx.enter_context(nc.sbuf_tensor("expert_ring", [P, self.PLACES, 4, D], F32))
        self.rows = ctx.enter_context(nc.sbuf_tensor("bias_rows", [1, 3, D], F32))
        self.landed = [ctx.enter_context(nc.semaphore(f"expert_landed{i}")) for i in range(self.PLACES)]
        self.gu_rows_in = ctx.enter_context(nc.semaphore("gate_up_bias_in"))
        self.d_row_in = ctx.enter_context(nc.semaphore("down_bias_in"))

    def load(self, sp, place, e):
        w = self.A[("w_gate_2", "w_up_2", "w_down_2")[place // 2]][0]
        h = place % 2
        src = w[bass.ds(e, 1), h * HALF:(h + 1) * HALF, :].rearrange("a (k p) n -> p (a k) n", p=P)
        sp.dma_start(self.ring[:, place, :, :], src).then_inc(self.landed[place], 16)

    def gate_up_rows(self, sp, e):
        for m, name in enumerate(("b_gate_2", "b_up_2")):
            sp.dma_start(self.rows[0:1, m, :], self.A[name][0][bass.ds(e, 1), :]).then_inc(self.gu_rows_in, 16)

    def down_row(self, sp, e):
        sp.dma_start(self.rows[0:1, 2, :], self.A["b_down_2"][0][bass.ds(e, 1), :]).then_inc(self.d_row_in, 16)

    def prefetch(self, sp):
        self.gate_up_rows(sp, 0)
        for place in range(4):
            self.load(sp, place, 0)
        self.down_row(sp, 0)
        for place in range(4, 6):
            self.load(sp, place, 0)


def stage_experts(nc, A, G):
    X = G.experts
    with ExitStack() as ctx:
        def sb(name, shape, dt=F32):
            return ctx.enter_context(nc.sbuf_tensor(name, shape, dt))

        sem = G.sem
        ps = G.ps
        xg = sb("slot_x", [P, D])
        xT = sb("slot_xT", [P, KB, P])
        ids = sb("slot_ids", [P, 1], I32)
        bias = sb("expert_bias", [P, 3, D])
        gt = sb("gate_act", [P, D])
        up = sb("up_act", [P, D])
        sg = sb("gate_sigmoid", [P, D])
        hid = sb("hidden", [P, D])
        hT = sb("hiddenT", [P, KB, P])
        y = sb("slot_y", [P, D])
        tick = sb("tick", [1, 4])
        names = ("tick_ok ids_ok x_turned xT_ok g_done g_read gt_ok sg_ok u_done u_read step hid_ok h_turned hT_ok d_done "
                 "y_ok gu_bias_ok d_bias_ok up_ok").split()
        q = {x: sem("ex_" + x) for x in names}
        q["xg_in"] = G.xg_in
        q["xg_in"] = G.xg_in
        held = [sem(f"ex_held{i}") for i in range(3)]
        B_G, B_U, B_D, B_T = 0, 2, 4, 6
        block = ctx.enter_context(nc.Block())


        def loop(eng, body):
            last = eng.value_load(G.last_slot[0:1, 0:1], min_val=EXPERTS - 1, max_val=MAX_SLOTS - 1)
            body(1, True)
            with eng.Fori(2, last + 1) as i:
                body(i, False)
            return last

        @block.sync
        def _(sp):
            def expert(i):
                at = i if isinstance(i, int) else bass.ds(i, 1)
                src = G.slot_expert[0:1, at:at + 1] if isinstance(i, int) else G.slot_expert[0:1, at]
                return sp.value_load(src, min_val=0, max_val=EXPERTS - 1)

            def down(i, e):
                sp.wait_ge(q["d_bias_ok"], i)
                X.down_row(sp, e)
                sp.wait_ge(q["d_done"], i)
                for place in (4, 5):
                    X.load(sp, place, e)

            def body(i, first):
                e = expert(i)
                sp.wait_ge(q["gu_bias_ok"], i)
                X.gate_up_rows(sp, e)
                sp.wait_ge(q["g_done"], i)
                for place in (0, 1):
                    X.load(sp, place, e)
                sp.wait_ge(q["u_done"], i)
                for place in (2, 3):
                    X.load(sp, place, e)
                if not first:
                    down(i - 1, expert(i - 1))
            last = loop(sp, body)
            down(last, expert(last))

        @block.gpsimd
        def _(pool):
            def hold(kind, i):
                if not (isinstance(i, int) and i == 0):
                    pool.wait_ge(held[kind], i)
                nc.gpsimd.tensor_tensor(tick[:, kind + 1:kind + 2], tick[:, 0:1], tick[:, 0:1], ALU.add)\
                    .then_inc(held[kind], 1)

            def gather(i):
                at = slice(i, i + 1) if isinstance(i, int) else bass.ds(i, 1)
                nc.gpsimd.tensor_copy(ids[:], G.slot_tokens[:, at]).then_inc(q["ids_ok"], 1)
                pool.wait_ge(q["ids_ok"], i + 1)
                hold(0, i)
                nc.gpsimd.indirect_dma_start(xg[:], None, G.h_dram[:, :], bass.IndirectOffsetOnAxis(ids[:, 0:1], 0))\
                    .then_inc(q["xg_in"], 16)

            def gate_up_bias(i):
                pool.wait_ge(X.gu_rows_in, i * 32 + 32)
                hold(1, i)
                nc.gpsimd.partition_broadcast(bias[:, 0, :], X.rows[0:1, 0, :])
                nc.gpsimd.partition_broadcast(bias[:, 1, :], X.rows[0:1, 1, :]).then_inc(q["gu_bias_ok"], 1)

            def down_bias(i):
                pool.wait_ge(X.d_row_in, i * 16 + 16)
                hold(2, i)
                nc.gpsimd.partition_broadcast(bias[:, 2, :], X.rows[0:1, 2, :]).then_inc(q["d_bias_ok"], 1)

            def body(i, first):
                pool.wait_ge(q["x_turned"], i + 1)
                gather(i + 1)
                pool.wait_ge(q["u_read"], i)
                gate_up_bias(i)
                if not first:
                    pool.wait_ge(q["y_ok"], i - 1)
                    down_bias(i - 1)
            nc.gpsimd.memset(tick[:], 0.0).then_inc(q["tick_ok"], 1)
            pool.wait_ge(q["tick_ok"], 1)
            pool.wait_ge(G.h_out, 16 * T)
            gather(0)
            gate_up_bias(0)
            pool.wait_ge(q["x_turned"], 1)
            gather(1)
            down_bias(0)
            last = loop(pool, body)
            pool.wait_ge(q["y_ok"], last)
            down_bias(last)
            pool.wait_ge(q["xg_in"], last * 16 + 32)
            pool.wait_ge(G.y_out, last * 16 + 16)

        @block.scalar
        def _(act):
            def x_turned(i):
                act.wait_ge(q["x_turned"], i + 1)
                nc.scalar.copy(xT[:, 0:4].rearrange("p k n -> p (k n)"), ps[:, B_T, :])
                nc.scalar.copy(xT[:, 4:8].rearrange("p k n -> p (k n)"), ps[:, B_T + 1, :]).then_inc(q["xT_ok"], 1)

            def h_turned(i):
                act.wait_ge(q["h_turned"], i + 1)
                nc.scalar.copy(hT[:, 0:4].rearrange("p k n -> p (k n)"), ps[:, B_T, :])
                nc.scalar.copy(hT[:, 4:8].rearrange("p k n -> p (k n)"), ps[:, B_T + 1, :]).then_inc(q["hT_ok"], 1)

            def sigmoid(i):
                act.wait_ge(q["gt_ok"], i + 1)
                nc.scalar.activation(sg[:], gt[:], ACT.Sigmoid, scale=1.702).then_inc(q["sg_ok"], 1)

            def store(i):
                act.wait_ge(q["y_ok"], i + 1)
                act.dma_start(G.y_dram[bass.ds(i * CAP, CAP), :], y[:]).then_inc(G.y_out, 16)

            def body(i, first):
                h_turned(i - 1)
                sigmoid(i)
                x_turned(i + 1)
                store(i - 1)
            x_turned(0)
            sigmoid(0)
            x_turned(1)
            last = loop(act, body)
            h_turned(last)
            store(last)

        @block.tensor
        def _(pe):
            def turn(src, i, done):
                for k in range(KB):
                    m = nc.tensor.transpose(ps[:, B_T + k // 4, (k % 4) * P:(k % 4 + 1) * P], src[:, k * P:(k + 1) * P],
                                            G.ident[:])
                m.then_inc(q[done], 1)

            def turn_x(i, prologue=False):
                pe.wait_ge(q["xg_in"], i * 16 + 16)
                if not prologue:
                    pe.wait_ge(q["hT_ok"], i - 1)
                turn(xg, i, "x_turned")

            def turn_h(i, last=False):
                pe.wait_ge(q["hid_ok"], i + 1)
                pe.wait_ge(q["xT_ok"], i + 2)
                turn(hid, i, "h_turned")

            def product(lhs, bank, place, i, done):
                for k in range(KB):
                    if k % 4 == 0:
                        pe.wait_ge(X.landed[place + k // 4], i * 16 + 16)
                    for h in range(2):
                        m = nc.tensor.matmul(ps[:, bank + h, :], lhs[:, k, :],
                                             X.ring[:, place + k // 4, k % 4, h * HALF:(h + 1) * HALF],
                                             start=(k == 0), stop=(k == KB - 1))
                m.then_inc(q[done], 1)

            def down(i, free):
                pe.wait_ge(q["hT_ok"], i + 1)
                if free:
                    pe.wait_ge(q["y_ok"], i)
                product(hT, B_D, 4, i, "d_done")

            def body(i, first):
                pe.wait_ge(q["xT_ok"], i + 1)
                pe.wait_ge(q["g_read"], i)
                product(xT, B_G, 0, i, "g_done")
                turn_h(i - 1)
                pe.wait_ge(q["u_read"], i)
                product(xT, B_U, 2, i, "u_done")
                turn_x(i + 1)
                down(i - 1, not first)
            turn_x(0, True)
            pe.wait_ge(q["xT_ok"], 1)
            product(xT, B_G, 0, 0, "g_done")
            product(xT, B_U, 2, 0, "u_done")
            turn_x(1, True)
            last = loop(pe, body)
            turn_h(last)
            down(last, True)

        @block.vector
        def _(dve):
            def two(ap):
                return ap.rearrange("p (h n) -> p h n", h=2)

            def hidden(i, very_first=False):
                if not very_first:
                    dve.wait_ge(q["hid_ok"], i)
                dve.wait_ge(q["gu_bias_ok"], i + 1)
                dve.wait_ge(q["g_done"], i + 1)
                nc.vector.tensor_tensor(two(gt[:]), ps[:, B_G:B_G + 2, :], two(bias[:, 0, :]), ALU.add)\
                    .then_inc(q["g_read"], 1)
                dve.wait_ge(q["g_read"], i + 1)
                nc.vector.tensor_scalar(gt[:], gt[:], 7.0, None, ALU.min).then_inc(q["gt_ok"], 1)
                dve.wait_ge(q["u_done"], i + 1)
                nc.vector.tensor_tensor(two(up[:]), ps[:, B_U:B_U + 2, :], two(bias[:, 1, :]), ALU.add)\
                    .then_inc(q["u_read"], 1)
                dve.wait_ge(q["u_read"], i + 1)
                nc.vector.tensor_scalar(up[:], up[:], 7.0, -7.0, ALU.min, ALU.max).then_inc(q["up_ok"], 1)
                dve.wait_ge(q["up_ok"], i + 1)
                dve.wait_ge(q["sg_ok"], i + 1)
                nc.vector.tensor_tensor(gt[:], gt[:], sg[:], ALU.mult).then_inc(q["step"], 1)
                dve.wait_ge(q["step"], i + 1)
                nc.vector.scalar_tensor_tensor(out=hid[:], in0=up[:], scalar=1.0, in1=gt[:], op0=ALU.add, op1=ALU.mult)\
                    .then_inc(q["hid_ok"], 1)

            def result(i, first):
                dve.wait_ge(q["d_bias_ok"], i + 1)
                dve.wait_ge(q["d_done"], i + 1)
                if not first:
                    dve.wait_ge(G.y_out, i * 16)
                nc.vector.tensor_tensor(two(y[:]), ps[:, B_D:B_D + 2, :], two(bias[:, 2, :]), ALU.add)\
                    .then_inc(q["y_ok"], 1)

            def body(i, first):
                hidden(i)
                result(i - 1, first)
            hidden(0, True)
            last = loop(dve, body)
            result(last, False)


def stage_final(nc, A, G):
    TK = T * TOP_K
    with ExitStack() as ctx:
        def sb(name, shape, dt=F32):
            return ctx.enter_context(nc.sbuf_tensor(name, shape, dt))
        sem = G.sem
        yk = sb("choice_y", [P, 8, D])
        acc = sb("ffn_sum", [P, D])
        in_ = G.choice_in
        added, acc_step, out_done = sem("added"), sem("acc_step"), sem("out_done_all")
        ln = Norm(nc, ctx, G, "ln2b", A["ln2_g_2"][0:1, :], A["ln2_b_2"][0:1, :])
        block = ctx.enter_context(nc.Block())

        @block.sync
        def _(sp):
            ln.load(sp)
            for t in range(T):
                sp.wait_ge(ln.ready, t + 1)
                sp.dma_start(A["out"][0, t * P:(t + 1) * P, :], G.X[:, t, :]).then_inc(out_done, 16)
            sp.wait_ge(out_done, 16 * T)

        @block.gpsimd
        def _(pool):
            for c in range(TK):
                if c >= 8:
                    pool.wait_ge(added, c - 7)
                nc.gpsimd.indirect_dma_start(yk[:, c % 8, :], None, G.y_dram[:, :],
                                             bass.IndirectOffsetOnAxis(G.choice_row[:, c:c + 1], 0))\
                    .then_inc(in_[c % 8], 16)
            for t in range(T):
                ln.gain_shift(pool, t)

        @block.scalar
        def _(act):
            for t in range(T):
                ln.root(act, t)

        @block.vector
        def _(dve):
            for c in range(TK):
                t, k = c // TOP_K, c % TOP_K
                dve.wait_ge(in_[c % 8], 16 * (c // 8 + 1))
                if k:
                    dve.wait_ge(added, c)
                    nc.vector.scalar_tensor_tensor(out=acc[:], in0=yk[:, c % 8, :], scalar=G.gates[:, t, k:k + 1],
                                                   in1=acc[:], op0=ALU.mult, op1=ALU.add).then_inc(added, 1)
                else:
                    nc.vector.tensor_scalar(acc[:], yk[:, c % 8, :], G.gates[:, t, 0:1], None, ALU.mult).then_inc(added, 1)
                if k == TOP_K - 1:
                    dve.wait_ge(added, c + 1)
                    nc.vector.scalar_tensor_tensor(out=G.X[:, t, :], in0=G.X[:, t, :], scalar=ALPHA, in1=acc[:],
                                                   op0=ALU.mult, op1=ALU.add).then_inc(ln.u_ok, 1)
                    ln.moments(dve, t)
                    ln.norm(dve, t)

def make_shared(nc, ctx, A):
    def sb(name, shape, dt=F32):
        return ctx.enter_context(nc.sbuf_tensor(name, shape, dt))

    def sem(name):
        return ctx.enter_context(nc.semaphore(name))
    G = Shared()
    G.ps = ctx.enter_context(nc.psum_tensor("banks", [P, 8, HALF], F32))
    G.ident, G.tri, G.strict, G.ones, G.late = (sb(x, [P, P]) for x in ("ident", "tri", "strict", "ones", "late"))
    G.ident_bf, G.causal_bf, G.before_bf = (sb(x, [P, P], BF16) for x in ("ident_bf", "causal_bf", "before_bf"))
    G.pcol = sb("param_cols", [P, P])
    G.mod2 = sb("mod2_cols", [P, 2 * KB])
    G.c_act = sb("c_act", [P, KB])
    G.hT = sb("hT", [P, KB, S])
    G.sums_dram = nc.dram_tensor("running_sums", [32, S], F32)
    G.h_dram = nc.dram_tensor("h_rows", [S, D], F32)
    G.y_dram = nc.dram_tensor("expert_rows", [MAX_SLOTS * CAP, D], F32)
    G.h_out, G.y_out, G.y_zeroed = sem("h_out"), sem("y_out"), sem("y_zeroed")
    G.sums_out, G.decays_ok, G.dtf_in = sem("sums_out"), sem("decays_ok"), sem("dtf_in")
    G.gate_bias_in, G.xg_in = sem("gate_bias_in"), sem("xg_in")
    G.choice_in = [sem(f"choice_in{i}") for i in range(8)]
    return G


def run_stage(nc, A, G, stage, last=False):
    with ExitStack() as ctx:
        made = []

        def sem(name):
            made.append(ctx.enter_context(nc.semaphore(name)))
            return made[-1]
        G.sem = sem
        stage(nc, A, G)
        if not last:
            with nc.Block() as block:
                @block.sync
                def _(sp):
                    for s in made:
                        sp.sem_clear(s)


def build(nc, A):
    with ExitStack() as ctx:
        G = make_shared(nc, ctx, A)

        def sbc(c, name, shape, dt=F32):
            return c.enter_context(nc.sbuf_tensor(name, shape, dt))
        with ExitStack() as first:
            G.W = Weights(nc, first, A)
            with ExitStack() as gates:
                G.gate = sbc(gates, "gates", [P, 2, D])
                mixed = ExitStack()
                G.mixT = sbc(mixed, "mixT", [P, 2 * KB, S])
                with ExitStack() as m:
                    G.xbcT = sbc(m, "xbcT", [P, XB, S])
                    G.w_dtf = sbc(m, "w_dtf", [P, KB, 32])
                    G.head_rows = sbc(m, "head_rows", [P, 48])
                    G.d_col = sbc(m, "d_col", [P, KB])
                    G.dt = sbc(m, "dt", [P, T, 16])
                    G.av = sbc(m, "rates", [P, T, 32])
                    G.acs = sbc(m, "acs", [P, 64])
                    G.decays = sbc(m, "decays", [P, 128])
                    run_stage(nc, A, G, stage_prepare)
                    run_stage(nc, A, G, stage_streams)
                    run_stage(nc, A, G, stage_mixer)
                G.X = ctx.enter_context(nc.sbuf_tensor("X", [P, T, D], F32, side="right"))
                with ExitStack() as y:
                    G.Y = sbc(y, "Y1", [P, 2, D])
                    run_stage(nc, A, G, stage_out)
                mixed.close()
                run_stage(nc, A, G, stage_ffn)
            with ExitStack() as y:
                G.Y = sbc(y, "Y2", [P, 2, D])
                run_stage(nc, A, G, stage_second)
        G.gates = sbc(ctx, "choice_gates", [P, T, TOP_K])
        G.choice_row = sbc(ctx, "choice_row", [P, T * TOP_K], I32)
        G.slot_tokens = sbc(ctx, "slot_tokens", [P, LIST], I32)
        G.slot_expert = sbc(ctx, "slot_expert", [P, LIST], I32)
        G.last_slot = sbc(ctx, "last_slot", [P, 1], I32)
        with ExitStack() as e:
            G.experts = Experts(nc, e, A)
            run_stage(nc, A, G, stage_route)
            run_stage(nc, A, G, stage_experts)
        run_stage(nc, A, G, stage_final, last=True)


_INS = ['x', 'c', 'w_ada', 'b_ada', 'w_in', 'conv_w', 'conv_b', 'dt_bias', 'a_log', 'd_skip',
        'ssm_norm_w', 'f_bias', 'attn_norm_w', 'w_out', 'ln1_g', 'ln1_b', 'w_ff_in', 'w_ff_out',
        'ln2_g', 'ln2_b', 'w_in_2', 'b_in_2', 'sinks_2', 'ln_v_g_2', 'ln_v_b_2', 'w_spatial_2',
        'b_spatial_2', 'w_out_2', 'b_out_2', 'ln1_g_2', 'ln1_b_2', 'w_router_2', 'b_router_2',
        'w_gate_2', 'b_gate_2', 'w_up_2', 'b_up_2', 'w_down_2', 'b_down_2', 'ln2_g_2', 'ln2_b_2']
_OUTS = [((1, S, D), 'float32')]


def kernel(**inputs):
    import numpy as _np
    import concourse.bacc as _bacc
    from concourse import mybir as _mybir
    from concourse.bass_utils import run_bass_kernel_spmd as _run

    nc = _bacc.Bacc("TRN2", target_bir_lowering=False, num_devices=1)
    arrays, args = {}, {}
    for name in _INS:
        a = _np.ascontiguousarray(inputs[name])
        arrays[f"in_{name}_dram"] = a
        args[name] = nc.dram_tensor(f"in_{name}_dram", a.shape, _mybir.dt.from_np(a.dtype), kind="ExternalInput").ap()
    for i, (shape, dtype) in enumerate(_OUTS):
        dt = _mybir.dt.from_np(_np.dtype(dtype))
        args["out"] = nc.dram_tensor(f"out_{i}_dram", shape, dt, kind="ExternalOutput").ap()
    build(nc, args)
    r = _run(nc, [arrays], core_ids=[0])
    got = tuple(r.results[0][f"out_{i}_dram"] for i in range(len(_OUTS)))
    return got[0]
```
